# Optimizing a Trainium2 kernel written in Bass

```python
import math
import jax, jax.numpy as jnp
from jax import lax
import numpy as np

D_MODEL = 1024
BATCH = 1
SEQ = 1024
DEPTH = 1
DEC_BATCH = 1
DEC_SEQ = 64
PAST_LEN = 256

CHUNK = 64
W_MIX = 512
N_BRANCH = 3
POOL_WINDOWS = (2, 4, 8, 16)
POOL_GROUPS = len(POOL_WINDOWS)
POOL_GROUP_W = W_MIX // POOL_GROUPS
POOL_HIST = max(POOL_WINDOWS) - 1
SSM_GROUP_CH = 16
SSM_GROUPS = W_MIX // SSM_GROUP_CH
SSM_STATE = 64
DT_MIN = 1e-3
DT_MAX = 1e-1
FOX_HEADS = 8
FOX_HEAD_DIM = W_MIX // FOX_HEADS
Q_BLOCK = 128
FORGET_BIAS_INIT = 2.0
NEG_INF = -1e30
D_FF = 2816
CONV_W = 3
EPS = 1e-6

COL_POOL = 0
COL_SSM = W_MIX
COL_Q = 2 * W_MIX
COL_K = 3 * W_MIX
COL_V = 4 * W_MIX
COL_F = 5 * W_MIX
COL_GATE = 5 * W_MIX + FOX_HEADS
D_IN = COL_GATE + N_BRANCH * D_MODEL

kernel_name = "hybrid_pool_s5_fox_streaming_step"

def rmsnorm(x, g):
    x32 = x.astype(jnp.float32)
    y = x32 * lax.rsqrt(jnp.mean(x32 * x32, axis=-1, keepdims=True) + EPS)
    return (y * g.astype(jnp.float32)).astype(x.dtype)

def pool_mixer(u, hist, pos, w_pool, pool_scale):
    bn, L, _ = u.shape
    full = jnp.concatenate([hist.astype(u.dtype), u], axis=1)
    cs = jnp.concatenate([jnp.zeros((bn, 1, W_MIX), jnp.float32),
                          jnp.cumsum(full.astype(jnp.float32), axis=1)], axis=1)
    end = cs[:, POOL_HIST + 1:]
    means = []
    for g, w in enumerate(POOL_WINDOWS):
        lo, hi = g * POOL_GROUP_W, (g + 1) * POOL_GROUP_W
        start = cs[:, POOL_HIST + 1 - w: POOL_HIST + 1 - w + L, lo:hi]
        cnt = jnp.minimum(pos + 1, w).astype(jnp.float32)[None, :, None]
        means.append((end[:, :, lo:hi] - start) / cnt)
    d = jnp.concatenate(means, axis=-1) - u.astype(jnp.float32)
    y = jnp.einsum('blgc,gcd->blgd', d.reshape(bn, L, POOL_GROUPS, POOL_GROUP_W),
                   w_pool.astype(jnp.float32))
    y = y.reshape(bn, L, W_MIX) * pool_scale.astype(jnp.float32)
    return y.astype(u.dtype), full[:, -POOL_HIST:]

def ssm_mixer(u, s0_re, s0_im, lam_re, lam_im, log_dt, b_re, b_im, c_re, c_im, d_skip, w_glu, b_glu):
    bn, L, _ = u.shape
    f32 = jnp.float32
    lam = lax.complex(lam_re.astype(f32), lam_im.astype(f32))
    dt = jnp.exp(log_dt.astype(f32))[:, None]
    lam_bar = jnp.exp(lam * dt)
    b_mat = lax.complex(b_re.astype(f32), b_im.astype(f32))
    b_bar = ((lam_bar - 1.0) / lam)[..., None] * b_mat
    c_mat = lax.complex(c_re.astype(f32), c_im.astype(f32))
    u32 = u.astype(f32)
    ug = u32.reshape(bn, L, SSM_GROUPS, SSM_GROUP_CH)
    bu = jnp.einsum('gpc,blgc->blgp', b_bar, ug)
    s0 = lax.complex(s0_re.astype(f32), s0_im.astype(f32))
    bu = bu.at[:, 0].add(lam_bar * s0)
    a = jnp.broadcast_to(lam_bar, bu.shape)

    def combine(e1, e2):
        a1, b1 = e1
        a2, b2 = e2
        return a1 * a2, a2 * b1 + b2

    _, states = lax.associative_scan(combine, (a, bu), axis=1)
    y = jnp.einsum('gcp,blgp->blgc', c_mat, states).real.reshape(bn, L, W_MIX)
    y = y + d_skip.astype(f32) * u32
    y = jax.nn.gelu(y)
    y = y * jax.nn.sigmoid(y @ w_glu.astype(f32) + b_glu.astype(f32))
    s_last = states[:, -1]
    return y.astype(u.dtype), jnp.real(s_last), jnp.imag(s_last)

def fox_attention(q, k, v, c_q, c_k, q_pos):
    bn, lq = q.shape[:2]
    lk = k.shape[1]
    k_pos = jnp.arange(lk, dtype=jnp.int32)
    c_kT = jnp.transpose(c_k, (0, 2, 1))
    scale = FOX_HEAD_DIM ** -0.5

    def attend(blk):
        qb, cqb, pb = blk
        s = jnp.einsum('bqhd,bkhd->bhqk', qb, k).astype(jnp.float32) * scale
        s = s + jnp.transpose(cqb, (0, 2, 1))[..., None] - c_kT[:, :, None, :]
        s = jnp.where((k_pos[None, :] <= pb[:, None])[None, None], s, NEG_INF)
        p = jax.nn.softmax(s, axis=-1)
        return jnp.einsum('bhqk,bkhd->bqhd', p.astype(v.dtype), v)

    if lq > Q_BLOCK and lq % Q_BLOCK == 0:
        nb = lq // Q_BLOCK
        qb = jnp.moveaxis(q.reshape(bn, nb, Q_BLOCK, FOX_HEADS, FOX_HEAD_DIM), 1, 0)
        cqb = jnp.moveaxis(c_q.reshape(bn, nb, Q_BLOCK, FOX_HEADS), 1, 0)
        pb = q_pos.reshape(nb, Q_BLOCK)
        o = lax.map(attend, (qb, cqb, pb))
        return jnp.moveaxis(o, 0, 1).reshape(bn, lq, FOX_HEADS, FOX_HEAD_DIM)
    return attend((q, c_q, q_pos))

def conv_ffn(h, hist, w_up, conv_w, conv_b, w_down):
    L = h.shape[1]
    up = h @ w_up
    full = jnp.concatenate([hist.astype(up.dtype), up], axis=1)
    conv = conv_b + full[:, 0:L] * conv_w[0]
    for j in range(1, CONV_W):
        conv = conv + full[:, j:j + L] * conv_w[j]
    gate, val = jnp.split(conv, 2, axis=-1)
    y = (jax.nn.silu(gate) * val) @ w_down
    return y, full[:, -(CONV_W - 1):]

def run_layer(x, pos, pool_hist, s_re, s_im, k_past, v_past, logf_past, conv_hist,
              norm_mix_g, w_in, b_f, w_pool, pool_scale, lam_re, lam_im, log_dt,
              b_re, b_im, c_re, c_im, d_skip, w_glu, b_glu, w_branch, w_out,
              norm_ffn_g, w_up, conv_w, conv_b, w_down):
    bn, L, _ = x.shape
    h = rmsnorm(x, norm_mix_g)
    z = h @ w_in
    u_pool = z[..., COL_POOL:COL_SSM]
    u_ssm = z[..., COL_SSM:COL_Q]
    q = z[..., COL_Q:COL_K].reshape(bn, L, FOX_HEADS, FOX_HEAD_DIM)
    k = z[..., COL_K:COL_V].reshape(bn, L, FOX_HEADS, FOX_HEAD_DIM)
    v = z[..., COL_V:COL_F].reshape(bn, L, FOX_HEADS, FOX_HEAD_DIM)
    logf = jax.nn.log_sigmoid(z[..., COL_F:COL_GATE].astype(jnp.float32)
                              + b_f.astype(jnp.float32))
    gates = jax.nn.sigmoid(z[..., COL_GATE:].reshape(bn, L, N_BRANCH, D_MODEL))

    y_a, pool_new = pool_mixer(u_pool, pool_hist, pos, w_pool, pool_scale)
    y_b, s_re_new, s_im_new = ssm_mixer(u_ssm, s_re, s_im, lam_re, lam_im, log_dt,
                                        b_re, b_im, c_re, c_im, d_skip, w_glu, b_glu)
    if k_past is None:
        k_all, v_all, logf_all = k, v, logf
    else:
        k_all = jnp.concatenate([k_past.astype(k.dtype), k], axis=1)
        v_all = jnp.concatenate([v_past.astype(v.dtype), v], axis=1)
        logf_all = jnp.concatenate([logf_past.astype(jnp.float32), logf], axis=1)
    c_all = jnp.cumsum(logf_all, axis=1)
    y_c = fox_attention(q, k_all, v_all, c_all[:, -L:], c_all, pos).reshape(bn, L, W_MIX)

    branches = jnp.stack([y_a, y_b, y_c.astype(y_a.dtype)], axis=2)
    proj = jnp.einsum('blnw,nwd->blnd', branches, w_branch)
    merged = jnp.sum(gates.astype(proj.dtype) * proj, axis=2)
    x = x + (merged @ w_out).astype(x.dtype)

    ff, conv_new = conv_ffn(rmsnorm(x, norm_ffn_g), conv_hist, w_up, conv_w, conv_b, w_down)
    x = x + ff.astype(x.dtype)
    return x, (pool_new, s_re_new, s_im_new, k, v, logf, conv_new)

def _stack(states, i):
    return jnp.stack([s[i] for s in states], axis=0)

def setup_inputs(seed: int = 0) -> dict:
    key = jax.random.key(seed)
    ks = iter(jax.random.split(key, 40))
    f32 = jnp.float32

    def nrm(shape, scale):
        return scale * jax.random.normal(next(ks), shape, f32)

    lam_im_base = jnp.broadcast_to(jnp.pi * jnp.arange(SSM_STATE, dtype=f32),
                                   (DEPTH, SSM_GROUPS, SSM_STATE))
    return {
        "x_prompt": nrm((BATCH, SEQ, D_MODEL), 1.0),
        "x_sample": nrm((DEC_BATCH, DEC_SEQ, D_MODEL), 1.0),
        "cache_pool": nrm((DEPTH, DEC_BATCH, POOL_HIST, W_MIX), 1.0),
        "state_ssm_re": nrm((DEPTH, DEC_BATCH, SSM_GROUPS, SSM_STATE), 0.5),
        "state_ssm_im": nrm((DEPTH, DEC_BATCH, SSM_GROUPS, SSM_STATE), 0.5),
        "cache_k": nrm((DEPTH, DEC_BATCH, PAST_LEN, FOX_HEADS, FOX_HEAD_DIM), 1.0),
        "cache_v": nrm((DEPTH, DEC_BATCH, PAST_LEN, FOX_HEADS, FOX_HEAD_DIM), 1.0),
        "cache_logf": jax.nn.log_sigmoid(nrm((DEPTH, DEC_BATCH, PAST_LEN, FOX_HEADS), 1.0)
                                         + FORGET_BIAS_INIT),
        "cache_ffn_conv": nrm((DEPTH, DEC_BATCH, CONV_W - 1, 2 * D_FF), 1.0),
        "norm_mix_g": 1.0 + nrm((DEPTH, D_MODEL), 0.02),
        "w_in": nrm((DEPTH, D_MODEL, D_IN), D_MODEL ** -0.5),
        "b_f": FORGET_BIAS_INIT + nrm((DEPTH, FOX_HEADS), 0.1),
        "w_pool": nrm((DEPTH, POOL_GROUPS, POOL_GROUP_W, POOL_GROUP_W), POOL_GROUP_W ** -0.5),
        "pool_scale": 1.0 + nrm((DEPTH, W_MIX), 0.02),
        "lam_re": -0.5 + nrm((DEPTH, SSM_GROUPS, SSM_STATE), 0.01),
        "lam_im": lam_im_base + nrm((DEPTH, SSM_GROUPS, SSM_STATE), 0.01),
        "log_dt": jax.random.uniform(next(ks), (DEPTH, SSM_GROUPS), f32,
                                     minval=math.log(DT_MIN), maxval=math.log(DT_MAX)),
        "b_re": nrm((DEPTH, SSM_GROUPS, SSM_STATE, SSM_GROUP_CH), (2 * SSM_GROUP_CH) ** -0.5),
        "b_im": nrm((DEPTH, SSM_GROUPS, SSM_STATE, SSM_GROUP_CH), (2 * SSM_GROUP_CH) ** -0.5),
        "c_re": nrm((DEPTH, SSM_GROUPS, SSM_GROUP_CH, SSM_STATE), (2 * SSM_STATE) ** -0.5),
        "c_im": nrm((DEPTH, SSM_GROUPS, SSM_GROUP_CH, SSM_STATE), (2 * SSM_STATE) ** -0.5),
        "d_skip": nrm((DEPTH, W_MIX), 0.5),
        "w_glu": nrm((DEPTH, W_MIX, W_MIX), W_MIX ** -0.5),
        "b_glu": nrm((DEPTH, W_MIX), 0.01),
        "w_branch": nrm((DEPTH, N_BRANCH, W_MIX, D_MODEL), W_MIX ** -0.5),
        "w_out": nrm((DEPTH, D_MODEL, D_MODEL), D_MODEL ** -0.5),
        "norm_ffn_g": 1.0 + nrm((DEPTH, D_MODEL), 0.02),
        "w_up": nrm((DEPTH, D_MODEL, 2 * D_FF), D_MODEL ** -0.5),
        "conv_w": nrm((DEPTH, CONV_W, 2 * D_FF), CONV_W ** -0.5),
        "conv_b": nrm((DEPTH, 2 * D_FF), 0.01),
        "w_down": nrm((DEPTH, D_FF, D_MODEL), D_FF ** -0.5),
        "norm_final_g": 1.0 + nrm((D_MODEL,), 0.02),
    }

def reference(x_prompt, x_sample, cache_pool, state_ssm_re, state_ssm_im, cache_k, cache_v,
              cache_logf, cache_ffn_conv, norm_mix_g, w_in, b_f, w_pool, pool_scale, lam_re,
              lam_im, log_dt, b_re, b_im, c_re, c_im, d_skip, w_glu, b_glu, w_branch, w_out,
              norm_ffn_g, w_up, conv_w, conv_b, w_down, norm_final_g):
    bp, lp, _ = x_prompt.shape
    ls = x_sample.shape[1]
    past = cache_k.shape[2]
    pos_p = jnp.arange(lp, dtype=jnp.int32)
    pos_s = past + jnp.arange(ls, dtype=jnp.int32)
    zero_pool = jnp.zeros((bp, POOL_HIST, W_MIX), x_prompt.dtype)
    zero_s = jnp.zeros((bp, SSM_GROUPS, SSM_STATE), jnp.float32)
    zero_conv = jnp.zeros((bp, CONV_W - 1, 2 * D_FF), x_prompt.dtype)

    hp, hs = x_prompt, x_sample
    st_p, st_s = [], []
    for l in range(DEPTH):
        layer_params = (norm_mix_g[l], w_in[l], b_f[l], w_pool[l], pool_scale[l], lam_re[l],
                        lam_im[l], log_dt[l], b_re[l], b_im[l], c_re[l], c_im[l], d_skip[l],
                        w_glu[l], b_glu[l], w_branch[l], w_out[l], norm_ffn_g[l], w_up[l],
                        conv_w[l], conv_b[l], w_down[l])
        hp, sp = run_layer(hp, pos_p, zero_pool, zero_s, zero_s, None, None, None, zero_conv,
                           *layer_params)
        hs, ss = run_layer(hs, pos_s, cache_pool[l], state_ssm_re[l], state_ssm_im[l],
                           cache_k[l], cache_v[l], cache_logf[l], cache_ffn_conv[l],
                           *layer_params)
        st_p.append(sp)
        st_s.append(ss)

    y_prompt = rmsnorm(hp, norm_final_g)
    y_sample = rmsnorm(hs, norm_final_g)
    return (y_prompt, y_sample,
            _stack(st_p, 0), _stack(st_s, 0),
            _stack(st_p, 1), _stack(st_s, 1),
            _stack(st_p, 2), _stack(st_s, 2),
            _stack(st_p, 3), _stack(st_s, 3),
            _stack(st_p, 4), _stack(st_s, 4),
            _stack(st_p, 5), _stack(st_s, 5),
            _stack(st_p, 6), _stack(st_s, 6))


_drawn_inputs = setup_inputs


def setup_inputs(seed=0):
    import zlib

    import numpy as np

    out = dict(_drawn_inputs(seed))
    spreads = {}
    factors = {'cache_logf': 39.696,
     'norm_mix_g': 2.828,
     'pool_scale': 6.15,
     'lam_re': 50.547,
     'w_glu': 2.985,
     'b_glu': 200.0,
     'norm_ffn_g': 7.634,
     'conv_b': 23.044,
     'norm_final_g': 24.494,
     'cache_k': 4.643,
     'cache_v': 6.758,
     'c_re': 7.31,
     'c_im': 7.57}
    for name, (base, spread) in spreads.items():
        noise = np.random.default_rng([zlib.crc32(name.encode()), seed]).standard_normal(out[name].shape)
        drawn = base * np.exp(spread * noise) if base else spread * noise
        out[name] = __import__('jax').numpy.asarray(drawn.astype(out[name].dtype))
    for name, factor in factors.items():
        out[name] = (out[name] * factor).astype(out[name].dtype)
    return out
```

```python
from contextlib import ExitStack
import math

import concourse.bass as bass
from concourse import mybir

F32, F32R = mybir.dt.float32, mybir.dt.float32r
ALU, ACT, AX = mybir.AluOpType, mybir.ActivationFunctionType, mybir.AxisListType

P = 128
D = 1024
TP, TS, PAST = 1024, 64, 256
T = TP + TS
TK = T + PAST
KD = D // P
W = 512
MW = W // P
HEADS, HD = 8, 64
GROUPS = ((0, 364), (364, 364), (728, 360))
TOK = [(128 * j, 128) for j in range(8)] + [(1024, 64)]
WINDOWS = (2, 4, 8, 16)
HIST = 15
FF = 2816
NF = FF // P
EPS = 1e-6
C = 16
NCH = T // C
NP_CH, NS_CH = TP // C, TS // C
G32, SC, SS = 32, 16, 64
NB = 8
E70 = NP_CH + 1 + NS_CH + 1


class Steps:

    def __init__(self, sem, names, loop=False):
        self.sem, self.names, self.loop, self.n = sem, list(names), loop, 0
        self.index = {n: k for k, n in enumerate(self.names)}
        assert len(self.index) == len(self.names)

    def credit(self):
        return self.sem, len(self.names)

    def mark(self, name):
        assert self.names[self.n % len(self.names)] == name, (self.names[self.n % len(self.names)], name)
        self.n += 1
        return self.sem, 1

    def at(self, name, i=0, before=0):
        size = len(self.names)
        return self.sem, i * size + (self.index[name] + 1 + (size * (1 - before) if self.loop else 0))


class StageSems:

    FIRST = 150

    def __init__(self, nc):
        self.nc, self.held = nc, []

    def __call__(self, name):
        self.held.append(self.nc.alloc_semaphore(name, num=self.FIRST + len(self.held)))
        return self.held[-1]

    def close(self):
        self.nc.all_engine_barrier(sems_to_clear=range(self.FIRST, self.FIRST + len(self.held)))
        for s in self.held:
            self.nc.release_semaphore(s)


def column_blocks(w, tiles):
    return w.rearrange("(k p) n -> p k n", p=P, k=tiles)


def gate_columns(io):
    return column_blocks(io["w_in"][0, :, 5 * W + HEADS:5 * W + HEADS + 3 * D], KD)


def split_weights(pool, n_pairs, buf, s, first=0):
    if not first:
        pool.sem_inc(s.w_split, 2)
    with pool.Fori(first, n_pairs) as i:
        for a in range(2):
            pool.wait_ge(s.raw_ld[a], 16 * i + 16)
            pool.wait_ge(s.mm_done, 2 * i + (a + 1))
            pool.sem_inc(buf.pool_tick, 1)
            pool.tensor_copy(buf.wh[:, a], buf.raw[:, a]).then_inc(s.w_hi, 1)
            pool.wait_ge(s.w_hi, 2 * i + (a + 1))
            pool.tensor_tensor(buf.wl[:, a], buf.raw[:, a], buf.wh[:, a].bitcast(F32),
                               ALU.subtract).then_inc(s.w_split, 1)


def prefetch_blocks(eng, m, nxt, sources, own=None, own_blocks=0):
    if own:
        eng.wait_ge(own.w_split, own_blocks + 2)
    for a, (src, shape) in enumerate(sources):
        eng.dma_start(shape(m.raw[:, a]), src).then_inc(nxt.raw_ld[a], 16)


def prefetch_split(pool, m, nxt, own=None, own_matmuls=0):
    pool.sem_inc(nxt.w_split, 2)
    if own:
        pool.wait_ge(own.mm_done, own_matmuls + 2)
    for a in range(2):
        pool.wait_ge(nxt.raw_ld[a], 16)
        pool.tensor_copy(m.wh[:, a], m.raw[:, a]).then_inc(nxt.w_hi, 1)
        pool.wait_ge(nxt.w_hi, a + 1)
        pool.tensor_tensor(m.wl[:, a], m.raw[:, a], m.wh[:, a].bitcast(F32), ALU.subtract).then_inc(nxt.w_split, 1)


def whole(raw):
    return raw


def two_tiles(raw):
    return raw.rearrange("p (k o) c -> p k (o c)", k=MW)


class WeightSems:

    def __init__(self, sem, tag):
        self.raw_ld = [sem(f"{tag}_raw_ld{a}") for a in range(2)]
        self.w_split, self.w_hi, self.mm_done = sem(f"{tag}_w_split"), sem(f"{tag}_w_hi"), sem(f"{tag}_mm_done")


def three_pass(pe, out, lhs, rhs, cols, first=True, last=True, ks=range(KD)):
    (wh, wl), (xh, xl) = lhs, rhs
    c0, cn = cols
    ks = list(ks)
    for k in ks:
        for n, (w, x) in enumerate(((wh, xh), (wh, xl), (wl, xh))):
            mm = pe.matmul(out, w(k), x(k)[:, c0:c0 + cn], start=first and k == ks[0] and n == 0,
                           stop=last and k == ks[-1] and n == 2)
    return mm



class NormSems:
    def __init__(self, sem, tag):
        (self.sq_ready, self.sq_used, self.sum_done, self.root_done, self.inv_done, self.nt_ready, self.hi_ready,
         self.lo_ready) = (sem(f"{tag}_{n}") for n in ("sq_ready", "sq_used", "sum_done", "root_done", "inv_done",
                                                      "nt_ready", "hi_ready", "lo_ready"))


class NormBuffers:
    def __init__(self, sq, acc, inv, nt, ss):
        self.sq, self.acc, self.inv, self.nt, self.ss = sq, acc, inv, nt, ss


def norm_buffers(sb, tag, ss):
    return NormBuffers(sb(f"{tag}_sq", [P, 2, T]), sb(f"{tag}_acc", [P, T]), sb(f"{tag}_inv", [P, T]),
                       sb(f"{tag}_nt", [P, 2, T]), ss)


def norm_scalar(act, m, b, s, split=True, squares=True):
    for k in range(KD if squares else 0):
        if k >= 3:
            act.wait_ge(s.sq_used, k - 2)
        act.activation(b.acc[:] if k == 0 else b.sq[:, k % 2], m.xt[:, k], ACT.Square).then_inc(s.sq_ready, 1)
    for g, (c0, cn) in enumerate(GROUPS):
        act.wait_ge(s.sum_done, g + 1)
        act.activation(b.inv[:, c0:c0 + cn], b.ss[:, g, 0:cn], ACT.Sqrt, scale=1.0 / D,
                       bias=m.eps[:, 0:1]).then_inc(s.root_done, 1)
    for k in range(KD if split else 0):
        act.wait_ge(s.nt_ready, k + 1)
        act.activation(m.hh[:, k], b.nt[:, k % 2], ACT.Copy).then_inc(s.hi_ready, 1)


def norm_tensor(pe, m, b, s, squares=KD - 1):
    pe.wait_ge(s.sq_used, squares)
    for g, (c0, cn) in enumerate(GROUPS):
        pe.matmul(b.ss[:, g, 0:cn], m.ones[:], b.acc[:, c0:c0 + cn], start=True, stop=True).then_inc(s.sum_done, 1)


def norm_vector(dve, m, b, s, gain, split=True, squares=True):
    for k in range(1, KD if squares else 0):
        dve.wait_ge(s.sq_ready, k + 1)
        if k > 1:
            dve.wait_ge(s.sq_used, k - 1)
        dve.tensor_tensor(b.acc[:], b.acc[:], b.sq[:, k % 2], ALU.add).then_inc(s.sq_used, 1)
    for g, (c0, cn) in enumerate(GROUPS):
        dve.wait_ge(s.root_done, g + 1)
        dve.reciprocal(b.inv[:, c0:c0 + cn], b.inv[:, c0:c0 + cn]).then_inc(s.inv_done, 1)
    dve.wait_ge(s.inv_done, len(GROUPS))
    if not split:
        for c0, c1 in ((0, TP // 2), (TP // 2, T)):
            for k in range(KD):
                x = m.xt[:, k, c0:c1]
                dve.scalar_tensor_tensor(out=x, in0=x, scalar=gain[:, k:k + 1], in1=b.inv[:, c0:c1],
                                         op0=ALU.mult, op1=ALU.mult).then_inc(s.nt_ready, 1)
        return

    def low(k):
        dve.wait_ge(s.hi_ready, k + 1)
        dve.wait_ge(s.nt_ready, k + 1)
        dve.tensor_tensor(m.hl[:, k], b.nt[:, k % 2], m.hh[:, k].bitcast(F32), ALU.subtract).then_inc(s.lo_ready, 1)

    for k in range(KD):
        if k >= 2:
            dve.wait_ge(s.lo_ready, k - 1)
        dve.scalar_tensor_tensor(out=b.nt[:, k % 2], in0=m.xt[:, k], scalar=gain[:, k:k + 1], in1=b.inv[:],
                                 op0=ALU.mult, op1=ALU.mult).then_inc(s.nt_ready, 1)
        if k:
            low(k - 1)
    low(KD - 1)



def stage_input(nc, m, io):
    with ExitStack() as ctx:
        sb = lambda n, s, d=F32: ctx.enter_context(nc.sbuf_tensor(n, s, d))
        ps = lambda n, s: ctx.enter_context(nc.psum_tensor(n, s, F32))
        sem = StageSems(nc)
        ctx.callback(sem.close)
        m.xt = sb("xt_in", [P, KD, T])
        rows = sb("vec_rows", [P, 4, P])
        xtok = sb("x_tok", [P, 2, D])
        vec_ps = ps("vec_ps", [P, 512])
        xps = [ps(f"x_ps{a}", [P, 2, 512]) for a in range(2)]
        b, s = norm_buffers(sb, "n1", ps("n1_ss", [P, 3, 512])), NormSems(sem, "n1")
        rows_ld, const, vec_done = sem("rows_ld"), sem("const_done"), sem("vec_done")
        x_ld, x_turned = [sem("x_ld0"), sem("x_ld1")], sem("x_turned")
        x_out = [sem("x_out0"), sem("x_out1")]
        xt_st, vec_out = sem("xt_st"), sem("vec_out")
        vecs = [
            (0, 0, 8, io["norm_mix_g"][0]), (0, 8, 8, io["norm_ffn_g"][0]), (0, 16, 8, io["norm_final_g"]),
            (0, 24, 4, io["pool_scale"][0]), (0, 28, 4, io["d_skip"][0]), (0, 32, 4, io["b_glu"][0]),
            (0, 36, 44, io["conv_b"][0]), (1, 0, 44, io["conv_w"][0, 0]), (1, 44, 44, io["conv_w"][0, 1]),
            (2, 0, 44, io["conv_w"][0, 2]), (3, 0, 44, io["cache_ffn_conv"][0, 0, 0]),
            (3, 44, 44, io["cache_ffn_conv"][0, 0, 1])]
        block = ctx.enter_context(nc.Block())

        @block.sync
        def _(sp):
            with sp.Fori(0, 4) as i:
                for a in range(2):
                    sp.wait_ge(x_turned, 2 * i + (a + 1))
                    sp.dma_start(xtok[:, a], io["x_prompt"][0, bass.ds((2 * i + a) * P, P), :]).then_inc(x_ld[a], 16)
            sp.wait_ge(x_turned, 9)
            sp.dma_start(xtok[0:TS, 0], io["x_sample"][0]).then_inc(x_ld[0], 16)
            sp.wait_ge(x_out[0], 6)
            sp.wait_ge(x_out[1], 5)
            sp.dma_start(m.xt_d, m.xt[:]).then_inc(xt_st, 16)
            sp.wait_ge(xt_st, 16)

        @block.gpsimd
        def _(pool):
            pool.memset(m.ident[:], 0.0).then_inc(const, 1)
            pool.memset(m.ones[:], 1.0).then_inc(const, 1)
            pool.memset(m.eps[:], EPS).then_inc(const, 1)
            pool.wait_ge(const, 3)
            pool.affine_select(out=m.ident[:], in_=m.ident[:], compare_op=ALU.not_equal, fill=1.0, base=0,
                               pattern=[[-1, P]], channel_multiplier=1).then_inc(const, 1)
            prefetch_split(pool, m, m.project_ws)

        @block.tensor
        def _(pe):
            pe.sem_inc(x_turned, 2)
            pe.wait_ge(const, 4)
            with pe.Fori(0, 4) as i:
                for a in range(2):
                    pe.wait_ge(x_ld[a], 16 * i + 16)
                    pe.wait_ge(x_out[a], i + 1)
                    for k in range(KD):
                        mm = pe.transpose(xps[a][:, k // 4, k % 4 * P:k % 4 * P + P], xtok[:, a, k * P:k * P + P],
                                          m.ident[:])
                    mm.then_inc(x_turned, 1)
            pe.wait_ge(x_ld[0], 80)
            pe.wait_ge(x_out[0], 5)
            for k in range(KD):
                mm = pe.transpose(xps[0][:, k // 4, k % 4 * P:k % 4 * P + TS], xtok[0:TS, 0, k * P:k * P + P],
                                  m.ident[0:TS, 0:TS])
            mm.then_inc(x_turned, 1)
            pe.wait_ge(rows_ld, 16 * len(vecs))
            for t, n in enumerate((80, 88, 44, 88)):
                mm = pe.transpose(vec_ps[:, 96 * t:96 * t + n], rows[0:n, t], m.ident[0:n, 0:n])
            mm.then_inc(vec_done, 1)
            norm_tensor(pe, m, b, s)

        @block.scalar
        def _(act):
            for t, r0, n, src in vecs:
                act.dma_start(rows[r0:r0 + n, t], src.rearrange("(r c) -> r c", c=P)).then_inc(rows_ld, 16)
            w = column_blocks(io["w_in"][0], KD)
            prefetch_blocks(act, m, m.project_ws, [(w[:, :, a * P:(a + 1) * P], whole) for a in range(2)])
            act.sem_inc(x_out[0], 1)
            view = xps[0][:].rearrange("p b (k c) -> p (b k) c", c=P)
            with act.Fori(0, 4) as i:
                act.wait_ge(x_turned, 2 * i + 3)
                act.activation(m.xt[:, :, bass.ds(2 * i * P, P)], view, ACT.Copy).then_inc(x_out[0], 1)
            act.wait_ge(x_turned, 11)
            act.activation(m.xt[:, :, TP:T], view[:, :, 0:TS], ACT.Copy).then_inc(x_out[0], 1)
            act.wait_ge(x_out[0], 6)
            act.wait_ge(x_out[1], 5)
            norm_scalar(act, m, b, s)

        @block.vector
        def _(dve):
            dve.sem_inc(x_out[1], 1)
            view = xps[1][:].rearrange("p b (k c) -> p (b k) c", c=P)
            with dve.Fori(0, 4) as i:
                dve.wait_ge(x_turned, 2 * i + 4)
                dve.tensor_copy(m.xt[:, :, bass.ds((2 * i + 1) * P, P)], view).then_inc(x_out[1], 1)
            dve.wait_ge(vec_done, 1)
            for t, (n, dst) in enumerate(((80, m.vec), (88, m.cw01), (44, m.cw2), (88, m.chist))):
                dve.tensor_copy(dst[:], vec_ps[:, 96 * t:96 * t + n]).then_inc(vec_out, 1)
            dve.wait_ge(vec_out, 4)
            dve.wait_ge(x_out[0], 6)
            dve.wait_ge(x_out[1], 5)
            norm_vector(dve, m, b, s, m.vec[:, 0:8])



def stage_project(nc, m, io):
    with ExitStack() as ctx:
        sb = lambda n, s, d=F32: ctx.enter_context(nc.sbuf_tensor(n, s, d))
        ps = lambda n, s: ctx.enter_context(nc.psum_tensor(n, s, F32))
        sem = StageSems(nc)
        ctx.callback(sem.close)
        z = sb("z", [P, 2, T])
        zh, zl = sb("z_hi", [P, 2, T], F32R), sb("z_lo", [P, 2, T], F32R)
        tok = sb("z_tok", [P, 2, 9, P])
        tokh, tokl = sb("z_tok_hi", [P, 2, 9, P], F32R), sb("z_tok_lo", [P, 2, 9, P], F32R)
        acc = [ps(f"z_ps{a}", [P, 3, 512]) for a in range(2)]
        tr = [ps(f"z_tr{a}", [P, 512]) for a in range(2)]
        ws = m.project_ws
        ps_free = sem("z_ps_free")
        u_st, q_st, k_st, v_st = ([sem(f"{n}_st{a}") for a in range(2)] for n in "uqkv")
        q_hi, q_lo, k_hi, k_lo, v_hi, v_lo = (sem(f"{n}_part") for n in ("qh", "ql", "kh", "kl", "vh", "vl"))
        tr_done, tr_out = sem("z_tr_done"), sem("z_tr_out")
        tables = SsmTables(sb, sem, tr[0], tr[0], tr[1])
        w = column_blocks(io["w_in"][0], KD)
        block = ctx.enter_context(nc.Block())

        @block.sync
        def _(sp):
            with sp.Fori(1, 10) as i:
                for a in range(2):
                    sp.wait_ge(ws.w_split, 2 * i + (a + 1))
                    sp.dma_start(m.raw[:, a], w[:, :, bass.ds((2 * i + a) * P, P)]).then_inc(ws.raw_ld[a], 16)
            tables.store(sp, m)
            sp.wait_ge(tables.tab_st, 16)

        @block.gpsimd
        def _(pool):
            split_weights(pool, 10, m, ws, first=1)

        @block.tensor
        def _(pe):
            pe.sem_inc(ws.mm_done, 2)
            pe.sem_inc(tr_done, 6)
            tables.tensor(pe, m)

            def tile(t, a):
                pe.wait_ge(ws.w_split, t + 3)
                for g, cols in enumerate(GROUPS):
                    mm = three_pass(pe, acc[a][:, g, 0:cols[1]], (lambda k: m.wh[:, a, k], lambda k: m.wl[:, a, k]),
                                    (lambda k: m.hh[:, k], lambda k: m.hl[:, k]), cols)
                mm.then_inc(ws.mm_done, 1)

            with pe.Fori(0, 4) as i:
                for a in range(2):
                    pe.wait_ge(ps_free, 2 * i + (a + 1))
                    tile(2 * i + a, a)
            pe.wait_ge(ps_free, 10)
            with pe.Fori(0, 2) as i:
                for a in range(2):
                    pe.wait_ge(q_lo, 2 * i + (a + 1))
                    tile(2 * i + (8 + a), a)
            pe.wait_ge(q_lo, 6)
            with pe.Fori(0, 4) as i:
                for a in range(2):
                    pe.wait_ge(ps_free, 2 * i + (9 + a))
                    tile(2 * i + (12 + a), a)
                for a in range(2):
                    pe.wait_ge(ps_free, 2 * i + (11 + a))
                    for j in range(3):
                        job = 3 * a + j
                        pe.wait_ge(tr_out, 6 * i + (job + 1))
                        pe.sem_inc(m.pe_tick, 1)
                        for n, (c0, cn) in enumerate(TOK[4 * j:4 * j + 4]):
                            mm = pe.transpose(tr[job % 2][0:cn, n * P:n * P + P], z[:, a, c0:c0 + cn], m.ident[:])
                        mm.then_inc(tr_done, 1)

        @block.scalar
        def _(act):
            act.sem_inc(ps_free, 2)
            tables.load(act, io)
            tables.scalar(act)

            def out_of_psum(a, dst, done, scale=1.0):
                for g, (c0, cn) in enumerate(GROUPS):
                    ins = act.activation(dst[:, a, c0:c0 + cn], acc[a][:, g, 0:cn], ACT.Copy, scale=scale)
                ins.then_inc(done, 1)

            for a in range(2):
                act.sem_inc(u_st[a], 16)
            with act.Fori(0, 4) as i:
                for a in range(2):
                    act.wait_ge(ws.mm_done, 2 * i + (a + 3))
                    act.wait_ge(u_st[a], 16 * i + 16)
                    out_of_psum(a, z, ps_free)
                    act.wait_ge(ps_free, 2 * i + (a + 3))
                    act.dma_start(m.u_d[bass.ds((2 * i + a) * P, P), :], z[:, a]).then_inc(u_st[a], 16)
            for a in range(2):
                act.sem_inc(q_st[a], 32)
            with act.Fori(0, 2) as i:
                for a in range(2):
                    act.wait_ge(ws.mm_done, 2 * i + (a + 11))
                    act.wait_ge(q_st[a], 32 * i + 32)
                    out_of_psum(a, zh, q_hi, HD ** -0.5)
                    act.wait_ge(q_hi, 2 * i + (a + 1))
                    act.dma_start(m.qh_d[bass.ds((2 * i + a) * P, P), :], zh[:, a].bitcast(F32)).then_inc(q_st[a], 16)
                    act.wait_ge(q_lo, 2 * i + (a + 3))
                    act.dma_start(m.ql_d[bass.ds((2 * i + a) * P, P), :], zl[:, a].bitcast(F32)).then_inc(q_st[a], 16)
            for a in range(2):
                act.wait_ge(u_st[a], 80)
                act.wait_ge(q_st[a], 96)
                act.sem_inc(k_st[a], 64)
            with act.Fori(0, 2) as i:
                for a in range(2):
                    act.wait_ge(ws.mm_done, 2 * i + (a + 15))
                    act.wait_ge(tr_done, 6 * i + 3 * (a + 1))
                    act.wait_ge(k_st[a], 64 * i + 64)
                    out_of_psum(a, z, ps_free)
                    act.wait_ge(ps_free, 2 * i + (a + 11))
                    act.activation(zh[:, a], z[:, a], ACT.Copy).then_inc(k_hi, 1)
                    act.wait_ge(k_hi, 2 * i + (a + 1))
                    act.dma_start(m.kh_d[bass.ds((2 * i + a) * P, P), 0:T], zh[:, a].bitcast(F32)).then_inc(k_st[a], 16)
                for a in range(2):
                    act.wait_ge(k_lo, 2 * i + (a + 1))
                    act.dma_start(m.kl_d[bass.ds((2 * i + a) * P, P), 0:T], zl[:, a].bitcast(F32)).then_inc(k_st[a], 16)
                    act.wait_ge(tr_out, 6 * i + 3 * a + 5)
                    cols = bass.ds((2 * i + a) * P, P)
                    act.dma_start(m.k_p[:, cols].rearrange("(j p) c -> p j c", p=P), tok[:, a, 0:8]).then_inc(k_st[a], 16)
                    act.dma_start(m.k_s[:, cols], tok[0:TS, a, 8]).then_inc(k_st[a], 16)
            for a in range(2):
                act.wait_ge(k_st[a], 192)
                act.sem_inc(v_st[a], 96)
            with act.Fori(0, 2) as i:
                for a in range(2):
                    act.wait_ge(ws.mm_done, 2 * i + (a + 19))
                    act.wait_ge(tr_done, 6 * i + 3 * (a + 1) + 12)
                    out_of_psum(a, z, ps_free)
                for a in range(2):
                    act.wait_ge(tr_out, 6 * i + 3 * a + 17)
                    act.wait_ge(v_st[a], 96 * i + 96)
                    act.activation(tokh[:, a, 0:8], tok[:, a, 0:8], ACT.Copy)
                    act.activation(tokh[0:TS, a, 8], tok[0:TS, a, 8], ACT.Copy).then_inc(v_hi, 1)
                    act.wait_ge(v_hi, 2 * i + (a + 1))
                    act.wait_ge(v_lo, 2 * i + (a + 1))
                    cols = bass.ds((2 * i + a) * P, P)
                    for (dst_p, dst_s), src in (((m.v_p, m.v_s), tok), ((m.vh_d[0:TP], m.vh_d[TP:T]), tokh),
                                                ((m.vl_d[0:TP], m.vl_d[TP:T]), tokl)):
                        src = src[:].bitcast(F32)
                        act.dma_start(dst_p[:, cols].rearrange("(j p) c -> p j c", p=P),
                                      src[:, a, 0:8]).then_inc(v_st[a], 16)
                        act.dma_start(dst_s[:, cols], src[0:TS, a, 8]).then_inc(v_st[a], 16)
            for a in range(2):
                act.wait_ge(v_st[a], 288)

        @block.vector
        def _(dve):
            dve.sem_inc(q_lo, 2)
            tables.vector(dve)
            with dve.Fori(0, 2) as i:
                for a in range(2):
                    dve.wait_ge(q_hi, 2 * i + (a + 1))
                    for g, (c0, cn) in enumerate(GROUPS):
                        ins = dve.scalar_tensor_tensor(out=zl[:, a, c0:c0 + cn], in0=acc[a][:, g, 0:cn],
                                                       scalar=HD ** -0.5, in1=zh[:, a, c0:c0 + cn].bitcast(F32),
                                                       op0=ALU.mult, op1=ALU.subtract)
                        if g < 2:
                            continue
                        ins.then_inc(q_lo, 1)
            dve.sem_inc(tr_out, 2)

            def frames_out(i, a, base):
                for j in range(3):
                    job = 3 * a + j
                    n, cn = (4, P) if j < 2 else (1, TS)
                    dve.wait_ge(tr_done, 6 * i + (job + 7 + base))
                    dve.tensor_copy(tok[0:cn, a, 4 * j:4 * j + n],
                                    tr[job % 2][0:cn, 0:n * P].rearrange("p (j c) -> p j c", c=P)).then_inc(tr_out, 1)

            with dve.Fori(0, 2) as i:
                for a in range(2):
                    dve.wait_ge(k_hi, 2 * i + (a + 1))
                    dve.tensor_tensor(zl[:, a], z[:, a], zh[:, a].bitcast(F32), ALU.subtract).then_inc(k_lo, 1)
                for a in range(2):
                    dve.wait_ge(k_st[a], 64 * i + 64)
                    frames_out(i, a, 0)
            for a in range(2):
                dve.wait_ge(k_st[a], 192)
            with dve.Fori(0, 2) as i:
                for a in range(2):
                    dve.wait_ge(v_st[a], 96 * i + 96)
                    frames_out(i, a, 12)
                    dve.wait_ge(v_hi, 2 * i + (a + 1))
                    dve.tensor_tensor(tokl[:, a, 0:8], tok[:, a, 0:8], tokh[:, a, 0:8].bitcast(F32), ALU.subtract)
                    dve.tensor_tensor(tokl[0:TS, a, 8], tok[0:TS, a, 8], tokh[0:TS, a, 8].bitcast(F32),
                                      ALU.subtract).then_inc(v_lo, 1)



def stage_small(nc, m, io):
    with ExitStack() as ctx:
        sb = lambda n, s, d=F32: ctx.enter_context(nc.sbuf_tensor(n, s, d))
        ps = lambda n, s: ctx.enter_context(nc.psum_tensor(n, s, F32))
        sem = StageSems(nc)
        ctx.callback(sem.close)
        U0, S0 = HIST, HIST + TP + HIST
        UP = S0 + TS
        hist, ht = sb("pool_hist", [HIST, W]), sb("pool_hist_t", [P, MW, C])
        up, win = sb("up", [P, 2, UP]), sb("win", [P, 2, UP])
        d, dh, dl = sb("pool_d", [P, T]), sb("pool_dh", [P, T], F32R), sb("pool_dl", [P, T], F32R)
        yh, yl = sb("pool_yh", [P, 2, T], F32R), sb("pool_yl", [P, 2, T], F32R)
        ramp, rcnt = sb("ramp", [P, C]), sb("rcnt", [P, MW, C])
        wp = sb("wp", [P, MW, P])
        wph, wpl = sb("wp_hi", [P, MW, P], F32R), sb("wp_lo", [P, MW, P], F32R)
        pnew = sb("pool_new", [HIST, 2, W])
        wf, wfh, wfl = sb("wf", [P, KD, HEADS]), sb("wf_hi", [P, KD, HEADS], F32R), sb("wf_lo", [P, KD, HEADS], F32R)
        bf, clf = sb("bf", [HEADS, 1]), sb("clf", [P, 2, HEADS])
        f, fe, fn, fm = (sb(n, [HEADS, TK]) for n in ("f", "fe", "fn", "fm"))
        fout = sb("fout", [P, 9, HEADS])
        ck = sb("ck", [P, 2, W])
        cv, cvh, cvl = sb("cv", [P, 2, W]), sb("cvh", [P, 2, W], F32R), sb("cvl", [P, 2, W], F32R)
        ckh, ckl = sb("ckh", [P, MW, PAST], F32R), sb("ckl", [P, MW, PAST], F32R)
        acc = [ps(f"s_ps{a}", [P, 3, 512]) for a in range(2)]
        tb = [ps(f"s_tb{a}", [P, 512]) for a in range(2)]
        ld = {n: sem(f"{n}_ld") for n in ("hist", "up0", "up1", "wp", "wf", "bf", "clf", "ck", "cv")}
        st, y_st = sem("small_st"), [sem("y_st0"), sem("y_st1")]
        gs = range(MW)
        pool_did = Steps(sem("pool_did"), ["zero_hist0", "zero_hist1", "mask_ones", "mask"])
        pe_did = Steps(sem("pe_did"), ["hist_turned", "ck_turned", "forget_mm"] +
                       [f"{n}{g}" for g in gs for n in ("mix_mm", "new_turned")] + ["forget_turned"])
        act_did = Steps(sem("act_did"), ["wf_hi", "wp_hi", "cv_hi", "ck_hi", "d_hi0", "exp", "ln", "y_hi0"] +
                        [f"{n}{g}" for g in gs[1:] for n in ("d_hi", "y_hi")])
        windows = lambda g: [f"hist{g}"] + [f"win{g}_{k}" for k in range(g + 1)] + [f"{x}{g}" for x in ("d", "d_ramp", "d_start")]
        dve_did = Steps(sem("dve_did"), ["ramp"] + [f"cnt{g}" for g in gs] + ["rcnt", "wf_lo", "wp_lo", "cv_lo", "hist_out",
                        "clf_out", "ck_lo"] + windows(0) + ["forget_out", "abs", "d_lo0"] +
                        [n for g in gs[1:] for n in windows(g) + [f"y_lo{g - 1}", f"d_lo{g}"]] +
                        ["minus", "neg_p", "neg_s", "sums", "y_lo3", "new_p", "new_s", "forget_frames"])
        block = ctx.enter_context(nc.Block())

        @block.sync
        def _(sp):
            sp.dma_start(wf[:], column_blocks(io["w_in"][0, :, 5 * W:5 * W + HEADS], KD)).then_inc(ld["wf"], 16)
            sp.dma_start(hist[:], io["cache_pool"][0, 0]).then_inc(ld["hist"], 16)
            sp.dma_start(clf[:], io["cache_logf"][0, 0].rearrange("(j p) h -> p j h", p=P)).then_inc(ld["clf"], 16)
            sp.dma_start(bf[:], io["b_f"][0].rearrange("(h a) -> h a", a=1)).then_inc(ld["bf"], 16)
            sp.dma_start(wp[:], io["w_pool"][0].rearrange("g c e -> c g e")).then_inc(ld["wp"], 16)
            sp.dma_start(ck[:], io["cache_k"][0, 0].rearrange("(j p) h d -> p j (h d)", p=P)).then_inc(ld["ck"], 16)
            sp.dma_start(cv[:], io["cache_v"][0, 0].rearrange("(j p) h d -> p j (h d)", p=P)).then_inc(ld["cv"], 16)

            def store_mix(g):
                sp.wait_ge(*dve_did.at(f"y_lo{g}"))
                sp.dma_start(m.yh_d[0, g * P:(g + 1) * P], yh[:, g % 2].bitcast(F32)).then_inc(y_st[g % 2], 16)
                sp.dma_start(m.yl_d[0, g * P:(g + 1) * P], yl[:, g % 2].bitcast(F32)).then_inc(y_st[g % 2], 16)

            for g in gs:
                if g >= 2:
                    sp.wait_ge(*dve_did.at(f"d_start{g - 2}"))
                    sp.wait_ge(*pe_did.at(f"new_turned{g - 2}"))
                rows = m.u_d[g * P:(g + 1) * P]
                sp.dma_start(up[:, g % 2, U0:U0 + TP], rows[:, 0:TP]).then_inc(ld[f"up{g % 2}"], 16)
                sp.dma_start(up[:, g % 2, S0:UP], rows[:, TP:T]).then_inc(ld[f"up{g % 2}"], 16)
                if g >= 2:
                    store_mix(g - 2)
            w = gate_columns(io)
            prefetch_blocks(sp, m, m.gate_ws, [(w[:, :, a * P:(a + 1) * P], whole) for a in range(2)])
            store_mix(2)
            store_mix(3)
            sp.wait_ge(*dve_did.at("ck_lo"))
            for dst, src in ((m.kh_d, ckh), (m.kl_d, ckl)):
                sp.dma_start(dst[:, T:TK].rearrange("(m p) t -> p m t", p=P), src[:].bitcast(F32)).then_inc(st, 16)
            for dst, src in ((m.vh_d, cvh), (m.vl_d, cvl)):
                sp.dma_start(dst[T:TK].rearrange("(j p) c -> p j c", p=P), src[:].bitcast(F32)).then_inc(st, 16)
            sp.wait_ge(*dve_did.at("sums"))
            for c0, c1, s0 in ((0, TP, 0), (TP, T, TP + PAST), (T, TK, TP)):
                sp.dma_start(m.nc_d[:, c0:c1], f[:, s0:s0 + c1 - c0]).then_inc(st, 16)
            sp.wait_ge(*dve_did.at("forget_frames"))
            sp.dma_start(io["pool_p"][0, 0], pnew[:, 0]).then_inc(st, 16)
            sp.dma_start(io["pool_s"][0, 0], pnew[:, 1]).then_inc(st, 16)
            sp.dma_start(io["logf_p"][0, 0].rearrange("(j p) h -> p j h", p=P), fout[:, 0:8]).then_inc(st, 16)
            sp.dma_start(io["logf_s"][0, 0], fout[0:TS, 8]).then_inc(st, 16)
            sp.wait_ge(st, 16 * 11)
            for a in range(2):
                sp.wait_ge(y_st[a], 64)

        @block.gpsimd
        def _(pool):
            for a in range(2):
                pool.memset(up[:, a, 0:HIST], 0.0).then_inc(*pool_did.mark(f"zero_hist{a}"))
            pool.memset(fm[:], 1.0).then_inc(*pool_did.mark("mask_ones"))
            pool.wait_ge(*pool_did.at("mask_ones"))
            pool.memset(fm[:, TP:TP + 1], 0.0).then_inc(*pool_did.mark("mask"))
            prefetch_split(pool, m, m.gate_ws)

        @block.tensor
        def _(pe):
            pe.wait_ge(ld["hist"], 16)
            pe.wait_ge(ld["clf"], 16)
            for g in gs:
                pe.transpose(tb[0][:, C * g:C * g + HIST], hist[:, g * P:(g + 1) * P], m.ident[0:HIST, 0:HIST])
            for j in range(2):
                mm = pe.transpose(tb[1][0:HEADS, j * P:(j + 1) * P], clf[:, j], m.ident[:])
            mm.then_inc(*pe_did.mark("hist_turned"))
            pe.wait_ge(ld["ck"], 16)
            pe.wait_ge(*dve_did.at("clf_out"))
            for g in gs:
                for j in range(2):
                    mm = pe.transpose(tb[g // 2][:, g % 2 * PAST + j * P:g % 2 * PAST + (j + 1) * P],
                                      ck[:, j, g * P:(g + 1) * P], m.ident[:])
            mm.then_inc(*pe_did.mark("ck_turned"))
            pe.wait_ge(*dve_did.at("wf_lo"))
            for g, cols in enumerate(GROUPS):
                mm = three_pass(pe, acc[0][0:HEADS, g, 0:cols[1]], (lambda k: wfh[:, k], lambda k: wfl[:, k]),
                                (lambda k: m.hh[:, k], lambda k: m.hl[:, k]), cols)
            mm.then_inc(*pe_did.mark("forget_mm"))
            pe.wait_ge(*dve_did.at("wp_lo"))
            for g in gs:
                a = (g + 1) % 2
                pe.wait_ge(*dve_did.at(f"d_lo{g}"))
                pe.wait_ge(*dve_did.at(f"y_lo{g - 2}" if g >= 2 else "forget_out"))
                for n, cols in enumerate(GROUPS):
                    mm = three_pass(pe, acc[a][:, n, 0:cols[1]], (lambda k: wph[:, g], lambda k: wpl[:, g]),
                                    (lambda k: dh[:], lambda k: dl[:]), cols, ks=[0])
                mm.then_inc(*pe_did.mark(f"mix_mm{g}"))
                pe.wait_ge(*dve_did.at("ck_lo"))
                for n, c0 in enumerate((U0 + TP - HIST, UP - HIST)):
                    mm = pe.transpose(tb[n][0:HIST, g * P:(g + 1) * P], up[:, g % 2, c0:c0 + HIST], m.ident[:])
                mm.then_inc(*pe_did.mark(f"new_turned{g}"))
            pe.wait_ge(*dve_did.at("new_s"))
            for n, (c0, cn) in enumerate(TOK):
                s0 = c0 if n < 8 else TP + PAST
                mm = pe.transpose(tb[0][0:cn, HEADS * n:HEADS * (n + 1)], fn[:, s0:s0 + cn], m.ident[0:HEADS, 0:HEADS])
            mm.then_inc(*pe_did.mark("forget_turned"))

        @block.scalar
        def _(act):
            act.wait_ge(ld["wf"], 16)
            act.activation(wfh[:], wf[:], ACT.Copy).then_inc(*act_did.mark("wf_hi"))
            act.wait_ge(ld["wp"], 16)
            act.activation(wph[:], wp[:], ACT.Copy).then_inc(*act_did.mark("wp_hi"))
            act.wait_ge(ld["cv"], 16)
            act.activation(cvh[:], cv[:], ACT.Copy).then_inc(*act_did.mark("cv_hi"))
            act.wait_ge(*pe_did.at("ck_turned"))
            for n in range(2):
                ins = act.activation(ckh[:, 2 * n:2 * n + 2], tb[n][:].rearrange("p (g t) -> p g t", t=PAST), ACT.Copy)
            ins.then_inc(*act_did.mark("ck_hi"))
            for g in gs:
                a = (g + 1) % 2
                act.wait_ge(*dve_did.at(f"d_start{g}"))
                if g >= 1:
                    act.wait_ge(*pe_did.at(f"mix_mm{g - 1}"))
                act.activation(dh[:], d[:], ACT.Copy).then_inc(*act_did.mark(f"d_hi{g}"))
                if g == 0:
                    act.wait_ge(*dve_did.at("abs"))
                    act.activation(fe[:, 0:T], fe[:, 0:T], ACT.Exp).then_inc(*act_did.mark("exp"))
                    act.wait_ge(*act_did.at("exp"))
                    act.activation(fe[:, 0:T], fe[:, 0:T], ACT.Ln, bias=m.ones[0:HEADS, 0:1]).then_inc(*act_did.mark("ln"))
                act.wait_ge(*pe_did.at(f"mix_mm{g}"))
                if g >= 2:
                    act.wait_ge(y_st[g % 2], 32)
                for n, (c0, cn) in enumerate(GROUPS):
                    ins = act.activation(yh[:, g % 2, c0:c0 + cn], acc[a][:, n, 0:cn], ACT.Copy,
                                         scale=m.vec[:, 24 + g:25 + g])
                ins.then_inc(*act_did.mark(f"y_hi{g}"))

        @block.vector
        def _(dve):
            dve.tensor_tensor_scan(ramp[:], m.ones[:, 0:C], m.ones[:, 0:C], 0.0, ALU.mult,
                                   ALU.add).then_inc(*dve_did.mark("ramp"))
            dve.wait_ge(*dve_did.at("ramp"))
            for g in gs:
                dve.tensor_scalar(rcnt[:, g], ramp[:], float(WINDOWS[g]), None, ALU.min).then_inc(*dve_did.mark(f"cnt{g}"))
            dve.wait_ge(*dve_did.at("cnt3"))
            dve.reciprocal(rcnt[:], rcnt[:]).then_inc(*dve_did.mark("rcnt"))
            dve.wait_ge(*act_did.at("wf_hi"))
            dve.tensor_tensor(wfl[:], wf[:], wfh[:].bitcast(F32), ALU.subtract).then_inc(*dve_did.mark("wf_lo"))
            dve.wait_ge(*act_did.at("wp_hi"))
            dve.tensor_tensor(wpl[:], wp[:], wph[:].bitcast(F32), ALU.subtract).then_inc(*dve_did.mark("wp_lo"))
            dve.wait_ge(*act_did.at("cv_hi"))
            dve.tensor_tensor(cvl[:], cv[:], cvh[:].bitcast(F32), ALU.subtract).then_inc(*dve_did.mark("cv_lo"))
            dve.wait_ge(*pe_did.at("hist_turned"))
            dve.tensor_copy(ht[:, :, 0:HIST], tb[0][:, 0:MW * C].rearrange("p (g c) -> p g c", c=C)[:, :, 0:HIST]
                            ).then_inc(*dve_did.mark("hist_out"))
            dve.tensor_scalar(fn[:, TP:TP + PAST], tb[1][0:HEADS, 0:PAST], -1.0, None,
                              ALU.mult).then_inc(*dve_did.mark("clf_out"))
            dve.wait_ge(*act_did.at("ck_hi"))
            for n in range(2):
                ins = dve.tensor_tensor(ckl[:, 2 * n:2 * n + 2], tb[n][:].rearrange("p (g t) -> p g t", t=PAST),
                                        ckh[:, 2 * n:2 * n + 2].bitcast(F32), ALU.subtract)
            ins.then_inc(*dve_did.mark("ck_lo"))
            dve.wait_ge(*pool_did.at("zero_hist1"))
            dve.wait_ge(*dve_did.at("hist_out"))

            def mix_low(g):
                dve.wait_ge(*act_did.at(f"y_hi{g}"))
                for n, (c0, cn) in enumerate(GROUPS):
                    ins = dve.scalar_tensor_tensor(
                        out=yl[:, g % 2, c0:c0 + cn], in0=acc[(g + 1) % 2][:, n, 0:cn], scalar=m.vec[:, 24 + g:25 + g],
                        in1=yh[:, g % 2, c0:c0 + cn].bitcast(F32), op0=ALU.mult, op1=ALU.subtract)
                ins.then_inc(*dve_did.mark(f"y_lo{g}"))

            def forget_out():
                dve.wait_ge(*pe_did.at("forget_mm"))
                dve.wait_ge(ld["bf"], 16)
                for g, (c0, cn) in enumerate(GROUPS):
                    ins = dve.tensor_scalar(f[:, c0:c0 + cn], acc[0][0:HEADS, g, 0:cn], bf[:, 0:1], None, ALU.add)
                ins.then_inc(*dve_did.mark("forget_out"))
                dve.wait_ge(*dve_did.at("forget_out"))
                dve.scalar_tensor_tensor(out=fe[:, 0:T], in0=f[:, 0:T], scalar=-1.0, in1=f[:, 0:T], op0=ALU.mult,
                                         op1=ALU.min).then_inc(*dve_did.mark("abs"))

            for g, w in enumerate(WINDOWS):
                a = g % 2
                dve.wait_ge(ld[f"up{a}"], 32 * (g // 2) + 32)
                dve.tensor_copy(up[:, a, U0 + TP:S0], ht[:, g, 0:HIST]).then_inc(*dve_did.mark(f"hist{g}"))
                src, last = up[:, a], f"hist{g}"
                for k in range(g + 1):
                    dve.wait_ge(*dve_did.at(last))
                    lo, h = 2 ** (k + 1) - 1, 2 ** k
                    dve.tensor_tensor(win[:, k % 2, lo:UP], src[:, lo:UP], src[:, lo - h:UP - h],
                                      ALU.add).then_inc(*dve_did.mark(f"win{g}_{k}"))
                    src, last = win[:, k % 2], f"win{g}_{k}"
                dve.wait_ge(*dve_did.at(last))
                for c0, u0, cn in ((0, U0, TP), (TP, S0, TS)):
                    ins = dve.scalar_tensor_tensor(out=d[:, c0:c0 + cn], in0=src[:, u0:u0 + cn], scalar=1.0 / w,
                                                   in1=up[:, a, u0:u0 + cn], op0=ALU.mult, op1=ALU.subtract)
                ins.then_inc(*dve_did.mark(f"d{g}"))
                dve.wait_ge(*dve_did.at(f"d{g}"))
                dve.tensor_tensor(d[:, 0:C], src[:, U0:U0 + C], rcnt[:, g], ALU.mult).then_inc(*dve_did.mark(f"d_ramp{g}"))
                dve.wait_ge(*dve_did.at(f"d_ramp{g}"))
                dve.tensor_tensor(d[:, 0:C], d[:, 0:C], up[:, a, U0:U0 + C],
                                  ALU.subtract).then_inc(*dve_did.mark(f"d_start{g}"))
                if g:
                    mix_low(g - 1)
                else:
                    forget_out()
                dve.wait_ge(*act_did.at(f"d_hi{g}"))
                dve.tensor_tensor(dl[:], d[:], dh[:].bitcast(F32), ALU.subtract).then_inc(*dve_did.mark(f"d_lo{g}"))
            dve.tensor_scalar(f[:, 0:T], f[:, 0:T], 0.0, None, ALU.min).then_inc(*dve_did.mark("minus"))
            dve.wait_ge(*dve_did.at("minus"))
            dve.wait_ge(*act_did.at("ln"))
            dve.tensor_tensor(fn[:, 0:TP], fe[:, 0:TP], f[:, 0:TP], ALU.subtract).then_inc(*dve_did.mark("neg_p"))
            dve.tensor_tensor(fn[:, TP + PAST:TK], fe[:, TP:T], f[:, TP:T], ALU.subtract).then_inc(*dve_did.mark("neg_s"))
            dve.wait_ge(*dve_did.at("neg_s"))
            dve.wait_ge(*pool_did.at("mask"))
            dve.tensor_tensor_scan(f[:], fm[:], fn[:], 0.0, ALU.mult, ALU.add).then_inc(*dve_did.mark("sums"))
            mix_low(3)
            dve.wait_ge(*pe_did.at("new_turned3"))
            for n, name in enumerate(("new_p", "new_s")):
                dve.tensor_copy(pnew[:, n], tb[n][0:HIST]).then_inc(*dve_did.mark(name))
            dve.wait_ge(*pe_did.at("forget_turned"))
            dve.tensor_scalar(fout[:, 0:8], tb[0][:, 0:8 * HEADS].rearrange("p (j h) -> p j h", h=HEADS), -1.0, None,
                              ALU.mult)
            dve.tensor_scalar(fout[0:TS, 8], tb[0][0:TS, 8 * HEADS:9 * HEADS], -1.0, None,
                              ALU.mult).then_inc(*dve_did.mark("forget_frames"))



PR, PI, B1, B2, C1, C2, RC, RS = 0, C + 1, 2 * C + 2, 3 * C + 2, 4 * C + 2, 5 * C + 2, 6 * C + 2, 6 * C + 2 + E70
R16, S0T = RS + E70, RS + E70 + 1
NTAB = S0T + 1


class SsmTables:

    def __init__(self, sb, sem, lam_ps, cx_ps, cy_ps):
        self.tab = sb("tab_all", [P, G32, NTAB])
        self.lam_rows, self.c_rows = sb("lam_rows", [G32, 3, P]), sb("c_rows", [P, 2, MW, P])
        self.bx, self.by = sb("bx", [P, G32, SC]), sb("by", [P, G32, SC])
        self.small = [sb(n, [P, G32]) for n in ("lre", "lim", "dt", "fr", "fi", "den", "ea", "turn", "cos1", "sin1",
                                                "t1", "t2", "t3")]
        self.ang, self.big = sb("ang", [P, 2, G32]), sb("tab_tmp", [P, 4, G32, 32])
        self.lam_ps, self.cx_ps, self.cy_ps = lam_ps, cx_ps, cy_ps
        self.lam_ld, self.dt_ld, self.b_ld, self.c_ld = (sem(n) for n in ("lam_ld", "dt_ld", "b_ld", "c_ld"))
        self.tab_step, self.re_dt_ready, self.ang_ready, self.tab_ready, self.lam_out, self.tab_st = (
            sem(n) for n in ("tab_step", "re_dt_ready", "ang_ready", "tab_ready", "lam_out", "tab_st"))
        self.lam_turned, self.c_turned = sem("lam_turned"), sem("c_turned")
        self.act_did = Steps(sem("tab_act_did"), ["exp_dt", "exp_re", "exp_chunk", "sin"])

    def load(self, act, io):
        H = SS
        for n, (left, right) in enumerate(((io["lam_re"][0], io["lam_re"][0]), (io["lam_im"][0], io["lam_im"][0]),
                                           (io["state_ssm_re"][0, 0], io["state_ssm_im"][0, 0]))):
            act.dma_start(self.lam_rows[:, n, 0:SS], left).then_inc(self.lam_ld, 16)
            act.dma_start(self.lam_rows[:, n, SS:P], right).then_inc(self.lam_ld, 16)
        act.dma_start(self.small[2][:], io["log_dt"][0].partition_broadcast(P)).then_inc(self.dt_ld, 16)
        for n, srcs in enumerate(((io["c_re"], io["c_im"]), (io["c_im"], io["c_re"]))):
            for h, src in zip((0, H), srcs):
                act.dma_start(self.c_rows[:, n, :, h:h + SS], src[0].rearrange("(m g) c p -> (g c) m p", m=MW)
                             ).then_inc(self.c_ld, 16)
        for dst, srcs in ((self.bx, (io["b_re"], io["b_im"])), (self.by, (io["b_im"], io["b_re"]))):
            for h, src in zip((0, H), srcs):
                act.dma_start(dst[h:h + SS], src[0].rearrange("g p c -> p g c")).then_inc(self.b_ld, 16)

    def store(self, sp, m):
        sp.wait_ge(self.tab_ready, 1)
        sp.dma_start(m.tab_d, self.tab[:]).then_inc(self.tab_st, 16)

    def tensor(self, pe, m):
        pe.wait_ge(self.lam_ld, 96)
        for n in range(3):
            mm = pe.transpose(self.lam_ps[:, n * G32:(n + 1) * G32], self.lam_rows[:, n], m.ident[0:G32, 0:G32])
        mm.then_inc(self.lam_turned, 1)
        pe.wait_ge(self.c_ld, 64)
        pe.wait_ge(self.lam_out, 1)
        for n, out in enumerate((self.cx_ps, self.cy_ps)):
            for k in range(MW):
                mm = pe.transpose(out[:, k * P:(k + 1) * P], self.c_rows[:, n, k], m.ident[:])
        mm.then_inc(self.c_turned, 1)

    def scalar(self, act):
        lre, lim, dt, fr, fi, den, ea, turn, c1, s1, t1, t2, t3 = self.small
        act.wait_ge(self.dt_ld, 16)
        act.activation(dt[:], dt[:], ACT.Exp).then_inc(*self.act_did.mark("exp_dt"))
        act.wait_ge(self.re_dt_ready, 1)
        act.activation(ea[:], t1[:], ACT.Exp).then_inc(*self.act_did.mark("exp_re"))
        act.activation(self.tab[:, :, R16], t1[:], ACT.Exp, scale=float(C)).then_inc(*self.act_did.mark("exp_chunk"))
        act.wait_ge(self.ang_ready, 1)
        act.activation(self.ang[:], self.ang[:], ACT.Sin).then_inc(*self.act_did.mark("sin"))

    def vector(self, dve):
        TWO_PI = 2 * math.pi
        H1 = 6.28125
        H2 = math.ldexp(round(math.ldexp(TWO_PI - H1, 22)), -22)
        H3 = TWO_PI - H1 - H2
        MAGIC = 1.5 * 2 ** 23
        H = SS
        lre, lim, dt, fr, fi, den, ea, turn, c1, s1, t1, t2, t3 = self.small
        count = [0]

        def step(ins):
            ins.then_inc(self.tab_step, 1)
            count[0] += 1
            dve.wait_ge(self.tab_step, count[0])

        def tt(out, a, b, op):
            step(dve.tensor_tensor(out, a, b, op))

        def ts(out, a, x, op0, y=None, op1=None):
            if y is None:
                step(dve.tensor_scalar(out, a, x, None, op0))
            else:
                step(dve.tensor_scalar(out, a, x, y, op0, op1))

        def stt(out, a, x, b, op0, op1):
            step(dve.scalar_tensor_tensor(out=out, in0=a, scalar=x, in1=b, op0=op0, op1=op1))

        def renorm(c, s):
            tt(t1[:], c, c, ALU.mult)
            tt(t2[:], s, s, ALU.mult)
            tt(t1[:], t1[:], t2[:], ALU.add)
            ts(t1[:], t1[:], -0.5, ALU.mult, 1.5, ALU.add)
            tt(c, c, t1[:], ALU.mult)
            tt(s, s, t1[:], ALU.mult)

        def double(re, im, n):
            for k0 in range(0, n, 32):
                k = min(n - k0, 32)
                br, bi = (x[:, :, n:n + 1].to_broadcast([P, G32, k]) for x in (re, im))
                ar, ai = (x[:, :, 1 + k0:1 + k0 + k] for x in (re, im))
                p = [self.big[:, q, :, 0:k] for q in range(4)]
                dve.tensor_tensor(p[0], ar, br, ALU.mult)
                dve.tensor_tensor(p[1], ai, bi, ALU.mult)
                dve.tensor_tensor(p[2], ar, bi, ALU.mult)
                tt(p[3], ai, br, ALU.mult)
                dve.tensor_tensor(re[:, :, n + 1 + k0:n + 1 + k0 + k], p[0], p[1], ALU.subtract)
                tt(im[:, :, n + 1 + k0:n + 1 + k0 + k], p[2], p[3], ALU.add)

        dve.wait_ge(self.lam_turned, 1)
        step(dve.tensor_copy(lre[:], self.lam_ps[:, 0:G32]))
        step(dve.tensor_copy(lim[:], self.lam_ps[:, G32:2 * G32]))
        step(dve.tensor_copy(self.tab[:, :, S0T], self.lam_ps[:, 2 * G32:3 * G32]))
        dve.sem_inc(self.lam_out, 1)
        dve.wait_ge(*self.act_did.at("exp_dt"))
        tt(t1[:], lre[:], dt[:], ALU.mult)
        dve.sem_inc(self.re_dt_ready, 1)
        tt(turn[:], lim[:], dt[:], ALU.mult)
        for n in range(2):
            a = self.ang[:, n]
            ts(t2[:], turn[:], 1 / TWO_PI, ALU.mult, 0.25 * n, ALU.add)
            ts(t2[:], t2[:], MAGIC, ALU.add, -MAGIC, ALU.add)
            stt(a, t2[:], -H1, turn[:], ALU.mult, ALU.add)
            stt(a, t2[:], -H2, a, ALU.mult, ALU.add)
            stt(a, t2[:], -H3, a, ALU.mult, ALU.add)
            if n:
                ts(a, a, math.pi / 2, ALU.add)
        PIF = 3.1415925
        ts(self.ang[:], self.ang[:], PIF, ALU.min, -PIF, ALU.max)
        dve.sem_inc(self.ang_ready, 1)
        dve.wait_ge(*self.act_did.at("sin"))
        dve.wait_ge(*self.act_did.at("exp_chunk"))
        step(dve.tensor_copy(s1[:], self.ang[:, 0]))
        step(dve.tensor_copy(c1[:], self.ang[:, 1]))
        renorm(c1[:], s1[:])
        pr, pi = self.tab[:, :, PR:PR + C + 1], self.tab[:, :, PI:PI + C + 1]
        step(dve.memset(pr[:, :, 0:1], 1.0))
        step(dve.memset(pi[:, :, 0:1], 0.0))
        tt(pr[:, :, 1], ea[:], c1[:], ALU.mult)
        tt(pi[:, :, 1], ea[:], s1[:], ALU.mult)
        tt(den[:], lre[:], lre[:], ALU.mult)
        tt(t2[:], lim[:], lim[:], ALU.mult)
        tt(den[:], den[:], t2[:], ALU.add)
        step(dve.reciprocal(den[:], den[:]))
        ts(t1[:], pr[:, :, 1], -1.0, ALU.add)
        tt(fr[:], t1[:], lre[:], ALU.mult)
        tt(t2[:], pi[:, :, 1], lim[:], ALU.mult)
        tt(fr[:], fr[:], t2[:], ALU.add)
        tt(fi[:], pi[:, :, 1], lre[:], ALU.mult)
        tt(t2[:], t1[:], lim[:], ALU.mult)
        tt(fi[:], fi[:], t2[:], ALU.subtract)
        tt(fr[:], fr[:], den[:], ALU.mult)
        tt(fi[:], fi[:], den[:], ALU.mult)
        for n in (1, 2, 4, 8):
            double(pr, pi, n)
        rc, rs = self.tab[:, :, RC:RC + E70], self.tab[:, :, RS:RS + E70]
        for _ in range(4):
            tt(t1[:], c1[:], c1[:], ALU.mult)
            tt(t2[:], s1[:], s1[:], ALU.mult)
            tt(t3[:], c1[:], s1[:], ALU.mult)
            tt(c1[:], t1[:], t2[:], ALU.subtract)
            ts(s1[:], t3[:], 2.0, ALU.mult)
            renorm(c1[:], s1[:])
        step(dve.memset(rc[:, :, 0:1], 1.0))
        step(dve.memset(rs[:, :, 0:1], 0.0))
        step(dve.tensor_copy(rc[:, :, 1], c1[:]))
        step(dve.tensor_copy(rs[:, :, 1], s1[:]))
        for n in (1, 2, 4, 8, 16, 32):
            if n > 1:
                renorm(rc[:, :, n], rs[:, :, n])
            double(rc, rs, n)
        ts(rs[0:H, :, 0:NP_CH + 1], rs[0:H, :, 0:NP_CH + 1], -1.0, ALU.mult)
        for x in (rc, rs):
            step(dve.tensor_copy(x[:, :, NP_CH + 1:E70], x[:, :, 0:NS_CH + 1]))
        dve.wait_ge(self.b_ld, 64)
        ts(self.by[0:H], self.by[0:H], -1.0, ALU.mult)
        f = [x[:].unsqueeze(2).to_broadcast([P, G32, SC]) for x in (fr, fi)]
        q = [self.big[:, n, :, 0:SC] for n in range(4)]
        tt(q[0], self.bx[:], f[0], ALU.mult)
        tt(q[1], self.by[:], f[1], ALU.mult)
        tt(q[2], self.by[:], f[0], ALU.mult)
        tt(q[3], self.bx[:], f[1], ALU.mult)
        tt(self.tab[:, :, B1:B1 + SC], q[0], q[1], ALU.add)
        tt(self.tab[:, :, B2:B2 + SC], q[2], q[3], ALU.subtract)
        dve.wait_ge(self.c_turned, 1)
        by_group = lambda x: x.rearrange("p (g c) -> p g c", c=SC)
        step(dve.tensor_copy(self.tab[0:H, :, C1:C1 + SC], by_group(self.cx_ps[0:H])))
        ts(self.tab[H:P, :, C1:C1 + SC], by_group(self.cx_ps[H:P]), -1.0, ALU.mult)
        ts(self.tab[:, :, C2:C2 + SC], by_group(self.cy_ps[:]), -1.0, ALU.mult)
        dve.sem_inc(self.tab_ready, 1)



UNITS = 9
PIECES = {0: 0, 2: 1, 4: 2, 6: 3, 7: 4, 8: 5}


def stage_attention(nc, m, io):
    with ExitStack() as ctx:
        sb = lambda n, s, d=F32: ctx.enter_context(nc.sbuf_tensor(n, s, d))
        ps = lambda n, s: ctx.enter_context(nc.psum_tensor(n, s, F32))
        sem = StageSems(nc)
        ctx.callback(sem.close)
        GATES = 16
        qs = sb("qs", [P, 2, T], F32R)
        kh, kl = sb("kh", [P, 2, TK], F32R), sb("kl", [P, 2, TK], F32R)
        vh, vl = sb("vh", [P, 2, 11, HD], F32R), sb("vl", [P, 2, 11, HD], F32R)
        nck = sb("nck", [P, 2, TK])
        prob = sb("prob", [P, 2, TP])
        pth, ptl = sb("pt_hi", [P, 2, 8, 256], F32R), sb("pt_lo", [P, 2, 8, 256], F32R)
        oh, ol = sb("o_hi", [HD, 2, 256], F32R), sb("o_lo", [HD, 2, 256], F32R)
        gout = sb("gate_out", [P, 2, T])
        mask, maskr, identr = sb("mask", [P, 384]), sb("mask_r", [P, 384], F32R), sb("ident_r", [P, P], F32R)
        top, ntop, total, inv = (sb(n, [P, 2]) for n in ("top", "ntop", "total", "inv"))
        gp, sp_, pp, op = ps("gate_ps", [P, 3, 512]), ps("score_ps", [P, TP]), ps("turn_ps", [P, TP]), ps("o_ps", [P, 512])
        ws = m.gate_ws
        units = [(j, u) for j in range(2) for u in range(UNITS)]
        head_ld, v_ld, g_st, o_st = ([sem(f"{n}{a}") for a in range(2)] for n in ("head_ld", "v_ld", "gate_st", "o_st"))
        consts = sem("mask_done")
        pe_names, act_names, dve_names = [], [], []

        def following(j, u):
            return [(j, u + 1)] if u + 1 < UNITS else [(1, 0)] if j == 0 else []

        for j in range(2):
            for u in range(UNITS):
                q = u // 2 - 1
                if j == u == 0:
                    pe_names.append("score0_0")
                    dve_names += ["top0_0", "ntop0_0"]
                    act_names.append("exp0_0")
                for v in following(j, u):
                    pe_names.append("score%d_%d" % v)
                piece = PIECES.get(u)
                if piece is not None and piece % 3 < 2:
                    pe_names.append(f"gate_mm{j}_{piece}")
                if piece is not None:
                    act_names.append(f"gate{j}_{piece}")
                dve_names += [f"inv{j}_{u}", f"norm{j}_{u}"]
                for v in following(j, u):
                    dve_names += ["top%d_%d" % v, "ntop%d_%d" % v]
                if u % 2 == 0 and u >= 2:
                    pe_names.append(f"pv{j}_{q}")
                    act_names.append(f"o_hi{j}_{q}")
                    dve_names.append(f"o_lo{j}_{q}")
                pe_names.append(f"turn{j}_{u}")
                act_names.append(f"p_hi{j}_{u}")
                for v in following(j, u):
                    act_names.append("exp%d_%d" % v)
                dve_names.append(f"p_lo{j}_{u}")
            pe_names.append(f"pv{j}_4")
            act_names.append(f"o_hi{j}_4")
            dve_names.append(f"o_lo{j}_4")
        pe_did, act_did, dve_did = (Steps(sem(f"{e}_did"), n, loop=True)
                                    for e, n in (("pe", pe_names), ("act", act_names), ("dve", dve_names)))

        def unit(steps, name, n, i):
            j, u = divmod(n % (2 * UNITS), UNITS)
            return steps.at(f"{name}{j}_{u}", i, before=int(n < 0))

        def group(steps, name, n, i):
            j, q = divmod(n % 10, 5)
            return steps.at(f"{name}{j}_{q}", i, before=int(n < 0))

        def extent(u):
            return (P, u * P, 256 * (u // 2 + 1), 0) if u < 8 else (TS, TP, TS + PAST, TP)

        def key_blocks(u):
            if u < 8:
                return [(P * k, P, k) for k in range(2 * (u // 2 + 1))]
            return [(0, TS, 8), (TS, P, 9), (TS + P, P, 10)]

        w = gate_columns(io)
        block = ctx.enter_context(nc.Block())

        @block.sync
        def _(sp):
            with sp.Fori(0, 4) as i:
                for j in range(2):
                    h = 2 * i + j
                    sp.wait_ge(*group(pe_did, "pv", 5 * j + 4 - 10, i))
                    rows = bass.ds(h * HD, HD)
                    for half, src in ((0, m.qh_d), (1, m.ql_d)):
                        sp.dma_start(qs[HD * half:HD * half + HD, j].bitcast(F32), src[rows, :]).then_inc(head_ld[j], 16)
                    for half in range(2):
                        for dst, src in ((kh, m.kh_d), (kl, m.kl_d)):
                            sp.dma_start(dst[HD * half:HD * half + HD, j].bitcast(F32), src[rows, :]).then_inc(head_ld[j], 16)
                    sp.dma_start(nck[:, j], m.nc_d[bass.ds(h, 1), :].partition_broadcast(P)).then_inc(head_ld[j], 16)
                    for dst, src in ((vh, m.vh_d), (vl, m.vl_d)):
                        dst = dst[:].bitcast(F32)
                        by_tile = lambda r0, r1: src[r0:r1, rows].rearrange("(k p) d -> p k d", p=P)
                        sp.dma_start(dst[:, j, 0:8], by_tile(0, TP)).then_inc(v_ld[j], 16)
                        sp.dma_start(dst[0:TS, j, 8], src[TP:T, rows]).then_inc(v_ld[j], 16)
                        sp.dma_start(dst[:, j, 9:11], by_tile(T, TK)).then_inc(v_ld[j], 16)
                    for a in range(2):
                        sp.wait_ge(ws.w_split, 4 * i + (2 * j + a + 3))
                        sp.dma_start(m.raw[:, a], w[:, :, bass.ds((4 * i + (2 * j + a + 2)) * P, P)]
                                     ).then_inc(ws.raw_ld[a], 16)

        @block.gpsimd
        def _(pool):
            pool.memset(mask[:], 0.0).then_inc(consts, 1)
            pool.wait_ge(consts, 1)
            pool.affine_select(out=mask[:], in_=mask[:], compare_op=ALU.is_ge, fill=-1e30, base=P,
                               pattern=[[-1, 384]], channel_multiplier=1).then_inc(consts, 1)
            pool.wait_ge(consts, 2)
            pool.tensor_copy(maskr[:], mask[:]).then_inc(consts, 1)
            pool.tensor_copy(identr[:], m.ident[:]).then_inc(consts, 1)
            split_weights(pool, GATES // 2 + 1, m, ws, first=1)

        @block.tensor
        def _(pe):
            pe.sem_inc(*pe_did.credit())
            pe.sem_inc(ws.mm_done, 2)
            pe.wait_ge(consts, 4)

            def score(i, j, u):
                nq, q0, nk, k0 = extent(u)
                n = UNITS * j + u
                if u == 0:
                    pe.wait_ge(head_ld[j], 112 * i + 112)
                pe.wait_ge(*unit(dve_did, "top", n - 1, i))
                for c in range(0, nk, 512):
                    cn = min(512, nk - c)
                    out = sp_[0:nq, c:c + cn]
                    pe.matmul(out, qs[:, j, q0:q0 + nq], kh[:, j, k0 + c:k0 + c + cn], start=True, stop=False)
                    masked = c + cn == nk
                    mm = pe.matmul(out, qs[:, j, q0:q0 + nq], kl[:, j, k0 + c:k0 + c + cn], start=False, stop=not masked)
                if u < 8:
                    m0 = P * (1 - u % 2)
                    mm = pe.matmul(sp_[:, nk - 256:nk], identr[:], maskr[:, m0:m0 + 256], start=False, stop=True)
                else:
                    mm = pe.matmul(sp_[0:TS, 0:TS], identr[0:TS, 0:TS], maskr[0:TS, P:P + TS], start=False, stop=True)
                mm.then_inc(*pe_did.mark(f"score{j}_{u}"))

            def gate_piece(i, j, piece):
                a, g = divmod(piece, 3)
                n = 6 * j + piece - 3
                if g == 0:
                    pe.wait_ge(ws.w_split, 4 * i + (2 * j + a + 3))
                pe.wait_ge(*act_did.at(f"gate{n % 12 // 6}_{n % 6}", i, before=int(n < 0)))
                mm = three_pass(pe, gp[:, g, 0:GROUPS[g][1]], (lambda k: m.wh[:, a, k], lambda k: m.wl[:, a, k]),
                                (lambda k: m.hh[:, k], lambda k: m.hl[:, k]), GROUPS[g])
                mm.then_inc(*((ws.mm_done, 1) if g == 2 else pe_did.mark(f"gate_mm{j}_{piece}")))

            def turn(i, j, u):
                nq, _, nk, _ = extent(u)
                n = UNITS * j + u
                pe.wait_ge(*unit(dve_did, "norm", n, i))
                pe.sem_inc(m.pe_tick, 1)
                for k, (c, cn, _) in enumerate(key_blocks(u)):
                    mm = pe.transpose(pp[0:cn, k * P:k * P + nq], prob[0:nq, n % 2, c:c + cn], m.ident[0:nq, 0:nq])
                mm.then_inc(*pe_did.mark(f"turn{j}_{u}"))

            def pv(i, j, q):
                n, nq = 5 * j + q, (256 if q < 4 else TS)
                pe.wait_ge(*unit(dve_did, "p_lo", UNITS * j + (2 * q + 1 if q < 4 else 8), i))
                if q == 4:
                    pe.sem_inc(m.pe_tick, 1)
                if q == 0:
                    pe.sem_inc(m.pe_tick, 1)
                    pe.wait_ge(v_ld[j], 96 * i + 96)
                blocks = key_blocks(2 * q)
                for b, (_, cn, t) in enumerate(blocks):
                    for x, (v, p) in enumerate(((vh, pth), (vl, pth), (vh, ptl))):
                        mm = pe.matmul(op[0:HD, 0:nq], v[0:cn, j, t], p[0:cn, n % 2, b, 0:nq],
                                       start=b == 0 and x == 0, stop=b == len(blocks) - 1 and x == 2)
                mm.then_inc(*pe_did.mark(f"pv{j}_{q}"))

            with pe.Fori(0, 4) as i:
                for j in range(2):
                    for u in range(UNITS):
                        if j == u == 0:
                            score(i, 0, 0)
                        for v in following(j, u):
                            score(i, *v)
                        if u in PIECES:
                            gate_piece(i, j, PIECES[u])
                        if u % 2 == 0 and u >= 2:
                            pv(i, j, u // 2 - 1)
                        turn(i, j, u)
                    pv(i, j, 4)

        @block.scalar
        def _(act):
            act.sem_inc(*act_did.credit())
            for a in range(2):
                act.sem_inc(g_st[a], 16)
                act.sem_inc(o_st[a], 32)

            def exp(i, j, u):
                nq, _, nk, _ = extent(u)
                n = UNITS * j + u
                act.wait_ge(*unit(dve_did, "ntop", n, i))
                act.activation(prob[0:nq, n % 2, 0:nk], prob[0:nq, n % 2, 0:nk], ACT.Exp, bias=ntop[0:nq, n % 2:n % 2 + 1],
                               accum_out=total[0:nq, n % 2:n % 2 + 1]).then_inc(*act_did.mark(f"exp{j}_{u}"))

            def gate(i, j, piece):
                a, g = divmod(piece, 3)
                c0, cn = GROUPS[g]
                if g == 0:
                    act.wait_ge(g_st[a], 32 * i + (16 * j + 16))
                act.wait_ge(*((ws.mm_done, 4 * i + (2 * j + a + 3)) if g == 2 else pe_did.at(f"gate_mm{j}_{piece}", i)))
                act.activation(gout[:, a, c0:c0 + cn], gp[:, g, 0:cn], ACT.Tanh,
                               scale=0.5).then_inc(*act_did.mark(f"gate{j}_{piece}"))
                if g == 2:
                    act.wait_ge(*act_did.at(f"gate{j}_{piece}", i))
                    act.dma_start(m.gate_d[bass.ds((4 * i + 2 * j + a) * P, P), :], gout[:, a]).then_inc(g_st[a], 16)

            def prob_high(i, j, u):
                nq = extent(u)[0]
                n, q = UNITS * j + u, u // 2
                act.wait_ge(*unit(pe_did, "turn", n, i))
                slot, c0 = (5 * j + q) % 2, P * (u % 2)
                blocks = key_blocks(u)
                if u < 8:
                    nb = len(blocks)
                    ins = act.activation(pth[:, slot, 0:nb, c0:c0 + P],
                                         pp[:, 0:nb * P].rearrange("p (b c) -> p b c", c=P), ACT.Copy)
                else:
                    for b, (_, cn, _) in enumerate(blocks):
                        ins = act.activation(pth[0:cn, slot, b, 0:TS], pp[0:cn, b * P:b * P + TS], ACT.Copy)
                ins.then_inc(*act_did.mark(f"p_hi{j}_{u}"))

            def out_high(i, j, q):
                n, nq = 5 * j + q, (256 if q < 4 else TS)
                act.wait_ge(*group(pe_did, "pv", n, i))
                act.wait_ge(o_st[n % 2], 160 * i + (32 * (n // 2) + 32))
                act.activation(oh[:, n % 2, 0:nq], op[0:HD, 0:nq], ACT.Copy).then_inc(*act_did.mark(f"o_hi{j}_{q}"))

            def out_store(i, j, q):
                n, nq = 5 * j + q, (256 if q < 4 else TS)
                act.wait_ge(*group(dve_did, "o_lo", n, i))
                rows, cols = bass.ds((2 * i + j) * HD, HD), slice(256 * q, 256 * q + nq)
                for dst, src in ((m.yh_d, oh), (m.yl_d, ol)):
                    act.dma_start(dst[2, rows, cols], src[:, n % 2, 0:nq].bitcast(F32)).then_inc(o_st[n % 2], 16)

            with act.Fori(0, 4) as i:
                for j in range(2):
                    for u in range(UNITS):
                        if j == u == 0:
                            exp(i, 0, 0)
                        if u in PIECES:
                            gate(i, j, PIECES[u])
                        if u % 2 == 0 and u >= 2:
                            out_high(i, j, u // 2 - 1)
                        prob_high(i, j, u)
                        for v in following(j, u):
                            exp(i, *v)
                        if u % 2 == 0 and u >= 2:
                            out_store(i, j, u // 2 - 1)
                    out_high(i, j, 4)
                    out_store(i, j, 4)
            for a in range(2):
                act.wait_ge(g_st[a], 16 + 16 * GATES // 2)
                act.wait_ge(o_st[a], 32 + 160 * 4)

        @block.vector
        def _(dve):
            dve.sem_inc(*dve_did.credit())

            def row_max(i, j, u):
                nq, _, nk, k0 = extent(u)
                n = UNITS * j + u
                x = n % 2
                dve.wait_ge(*unit(pe_did, "score", n, i))
                dve.sem_inc(m.dve_tick, 1)
                dve.tensor_tensor_reduce(out=prob[0:nq, x, 0:nk], in0=sp_[0:nq, 0:nk], in1=nck[0:nq, j, k0:k0 + nk],
                                         scale=1.0, scalar=-3.0e38, op0=ALU.add, op1=ALU.max,
                                         accum_out=top[0:nq, x:x + 1]).then_inc(*dve_did.mark(f"top{j}_{u}"))
                dve.wait_ge(*dve_did.at(f"top{j}_{u}", i))
                dve.tensor_scalar(ntop[0:nq, x:x + 1], top[0:nq, x:x + 1], -1.0, None,
                                  ALU.mult).then_inc(*dve_did.mark(f"ntop{j}_{u}"))

            def normalise(i, j, u):
                nq, _, nk, _ = extent(u)
                x = (UNITS * j + u) % 2
                dve.wait_ge(*unit(act_did, "exp", UNITS * j + u, i))
                dve.reciprocal(inv[0:nq, x:x + 1], total[0:nq, x:x + 1]).then_inc(*dve_did.mark(f"inv{j}_{u}"))
                dve.wait_ge(*dve_did.at(f"inv{j}_{u}", i))
                dve.tensor_scalar(prob[0:nq, x, 0:nk], prob[0:nq, x, 0:nk], inv[0:nq, x:x + 1], None,
                                  ALU.mult).then_inc(*dve_did.mark(f"norm{j}_{u}"))

            def out_low(i, j, q):
                n, nq = 5 * j + q, (256 if q < 4 else TS)
                dve.wait_ge(*group(act_did, "o_hi", n, i))
                dve.tensor_tensor(ol[:, n % 2, 0:nq], op[0:HD, 0:nq], oh[:, n % 2, 0:nq].bitcast(F32),
                                  ALU.subtract).then_inc(*dve_did.mark(f"o_lo{j}_{q}"))

            def prob_low(i, j, u):
                n, q = UNITS * j + u, u // 2
                dve.wait_ge(*unit(act_did, "p_hi", n, i))
                slot, c0 = (5 * j + q) % 2, P * (u % 2)
                blocks = key_blocks(u)
                if u < 8:
                    nb = len(blocks)
                    ins = dve.tensor_tensor(ptl[:, slot, 0:nb, c0:c0 + P],
                                            pp[:, 0:nb * P].rearrange("p (b c) -> p b c", c=P),
                                            pth[:, slot, 0:nb, c0:c0 + P].bitcast(F32), ALU.subtract)
                else:
                    for b, (_, cn, _) in enumerate(blocks):
                        ins = dve.tensor_tensor(ptl[0:cn, slot, b, 0:TS], pp[0:cn, b * P:b * P + TS],
                                                pth[0:cn, slot, b, 0:TS].bitcast(F32), ALU.subtract)
                ins.then_inc(*dve_did.mark(f"p_lo{j}_{u}"))

            with dve.Fori(0, 4) as i:
                for j in range(2):
                    for u in range(UNITS):
                        if j == u == 0:
                            row_max(i, 0, 0)
                        normalise(i, j, u)
                        for v in following(j, u):
                            row_max(i, *v)
                        if u % 2 == 0 and u >= 2:
                            out_low(i, j, u // 2 - 1)
                        prob_low(i, j, u)
                    out_low(i, j, 4)



def stage_ssm(nc, m, io):
    with ExitStack() as ctx:
        sb = lambda n, s, d=F32: ctx.enter_context(nc.sbuf_tensor(n, s, d))
        ps = lambda n, s: ctx.enter_context(nc.psum_tensor(n, s, F32))
        sem = StageSems(nc)
        ctx.callback(sem.close)
        GATE0 = 16
        KW = (C - 1) * SC
        flat = lambda t: t[:].rearrange("p g e -> p (g e)")
        tab, ut = sb("tab", [P, 2, NB, NTAB]), sb("ut", [P, 2, T])
        uc = sb("uc", [NCH, NB, C, SC])
        yc = uc[:].rearrange("e g s c -> e (g s c)").rearrange("e (t c) -> e t c", c=P)
        u2 = sb("u2", [P, 2 * NB, NCH])
        w, wt = sb("ssm_w", [P, NB, C, SC]), sb("ssm_wt", [P, NB // 2, C, SC])
        cl = sb("cl", [P, NB, C + 1, SC])
        et = sb("et", [P, 2 * NB, P + 8])
        kp = sb("kp", [SC, NB, KW + C * SC])
        tm1, tm0 = sb("toeplitz1", [P, NB, C * SC]), sb("toeplitz0", [P, NB, C * SC // 2])
        vv, x1, x2, d0 = (sb(n, [P, NB, E70]) for n in ("vv", "x1", "x2", "d0"))
        ww = x2
        sc, sf = sb("sc", [P, NB, NCH]), sb("sf", [P, G32, 2])
        yt, gout = sb("yt", [P, T]), sb("gate_out3", [P, T])
        swap = sb("swap", [P, P])
        fin = flat(x1)[0:G32, 0:2 * P].rearrange("g (n c) -> g n c", n=2)
        r4, gp = ps("r4", [P, 4, 512]), ps("gate_ps3", [P, 3, 512])
        ws = m.gate_ws
        tab_ld, ut_ld = ([sem(f"{n}_ld{a}") for a in range(2)] for n in ("tab", "ut"))
        tm_ld, y_st, g_st, fin_st, consts, fin_mm, fin_out = (
            sem(n) for n in ("tm_ld", "y_st", "g_st", "fin_st", "consts", "fin_mm", "fin_out"))
        J = range(2)
        pe_did = Steps(sem("pe_did"), [f"{n}{j}" for j in J for n in (
            "uc", "gate0_", "u2", "gate1_", "et", "k", "v", "gate3_", "swap_v", "gate4_", "swap_w", "y", "back")], loop=True)
        act_did = Steps(sem("act_did"), [f"{n}{j}" for j in J for n in (
            "uc", "gate0_", "u2", "gate1_", "et", "gate2_", "kp", "s0_", "vv", "gate3_", "gate4_", "gate5_", "yc")], loop=True)
        dve_did = Steps(sem("dve_did"), [f"{n}{j}" for j in J for n in (
            "uc", "cl_a", "cl_b", "cl", "et", "d0", "kp", "x1", "x2", "d1", "ww", "x3", "x4", "sf", "sc", "yc", "yt")],
            loop=True)
        pool_did = Steps(sem("pool_did"), [f"{n}{j}" for j in J for n in ("w_a0", "w_b0", "w0_", "w_a1", "w_b1", "w")], loop=True)
        gate_w = gate_columns(io)
        uc_bank = lambda b: (uc[:, :, 4 * b:4 * b + 4].rearrange("e g s c -> e s g c"),
                             r4[0:NCH, b].rearrange("e (s g c) -> e s g c", s=4, c=SC))
        halves = lambda t: t[:].rearrange("p g e -> p (g e)").rearrange("p (b n) -> p b n", b=2)
        NSW = NB * E70 // 2
        swapped = r4[:, 0:2, 0:NSW]
        CS = C * SC
        block = ctx.enter_context(nc.Block())

        @block.sync
        def _(sp):
            def load(t):
                i, j = divmod(t, 2)
                sp.wait_ge(*pe_did.at(f"y{j}", i, before=1))
                sp.dma_start(tab[:, j], m.tab_d[:, t * NB:(t + 1) * NB]).then_inc(tab_ld[j], 16)
                sp.wait_ge(*dve_did.at(f"yt{j}", i, before=1))
                sp.dma_start(ut[:, j], m.u_d[W + t * P:W + (t + 1) * P]).then_inc(ut_ld[j], 16)
                for n in range(GATE0 + 2 * t, GATE0 + 2 * t + 2) if t else ():
                    sp.wait_ge(ws.w_split, n + 1)
                    sp.dma_start(m.raw[:, n % 2], gate_w[:, :, n * P:(n + 1) * P]).then_inc(ws.raw_ld[n % 2], 16)

            load(0)
            for t in range(MW):
                if t + 1 < MW:
                    load(t + 1)
                i, j = divmod(t, 2)
                sp.wait_ge(*act_did.at(f"kp{j}", i))
                sp.wait_ge(*dve_did.at(f"kp{j}", i))
                for r in range(C):
                    rows = slice(r % 8 * SC, (r % 8 + 1) * SC)
                    dst, c0, cn = (tm1, r * SC, CS) if r >= 8 else (tm0, r * SC + CS // 2, CS // 2)
                    sp.dma_start(dst[rows], kp[:, :, c0:c0 + cn]).then_inc(tm_ld, 16)
            prefetch_blocks(sp, m, m.merge_ws, [(column_blocks(io["w_branch"][0, 0], MW)[:, :, 2 * a * P:2 * (a + 1) * P],
                                                 two_tiles) for a in range(2)], ws, 24)
            sp.wait_ge(ws.mm_done, 26)
            for src, dst in ((m.yh_d, m.hh), (m.yl_d, m.hl)):
                sp.dma_start(dst[:, 0:MW].bitcast(F32), src[0].rearrange("(k p) t -> p k t", p=P)).then_inc(m.b0_ld, 16)
            sp.wait_ge(fin_out, 1)
            for n, (re, im) in enumerate(((io["ssm_re_p"], io["ssm_im_p"]), (io["ssm_re_s"], io["ssm_im_s"]))):
                sp.dma_start(re[0, 0], fin[:, n, 0:SS]).then_inc(fin_st, 16)
                sp.dma_start(im[0, 0], fin[:, n, SS:P]).then_inc(fin_st, 16)
            sp.wait_ge(fin_st, 64)

        @block.gpsimd
        def _(pool):
            pool.sem_inc(*pool_did.credit())
            for i in range(2):
                for j in J:
                    t = 2 * i + j
                    pool.wait_ge(tab_ld[j], 16 * i + 16)
                    if j == 0:
                        pool.wait_ge(*pe_did.at("et1", i, before=1))
                    else:
                        pool.wait_ge(*pe_did.at("et0", i))
                    pool.sem_inc(m.pool_tick, 1)
                    for h in range(2):
                        g = slice(4 * h, 4 * h + 4)
                        powers = lambda c: tab[:, j, g, c:c + C].unsqueeze(3).to_broadcast([P, 4, C, SC])
                        matrix = lambda c: tab[:, j, g, c:c + SC].unsqueeze(2).to_broadcast([P, 4, C, SC])
                        pool.tensor_tensor(w[:, g], powers(PR), matrix(B1), ALU.mult).then_inc(*pool_did.mark(f"w_a{h}{j}"))
                        pool.tensor_tensor(wt[:], powers(PI), matrix(B2), ALU.mult).then_inc(*pool_did.mark(f"w_b{h}{j}"))
                        pool.wait_ge(*pool_did.at(f"w_b{h}{j}", i))
                        pool.tensor_tensor(w[:, g], w[:, g], wt[:], ALU.add).then_inc(
                            *pool_did.mark(f"w{j}" if h else f"w0_{j}"))
                        if h == 0:
                            pool.wait_ge(*pool_did.at(f"w0_{j}", i))
                    for n in range(GATE0 + 2 * t + 2, GATE0 + 2 * t + 4) if t + 1 < MW else ():
                        a = n % 2
                        pool.wait_ge(ws.raw_ld[a], 16 * (n // 2 + 1))
                        pool.wait_ge(ws.mm_done, n + 1)
                        pool.tensor_copy(m.wh[:, a], m.raw[:, a]).then_inc(ws.w_hi, 1)
                        pool.wait_ge(ws.w_hi, n + 1)
                        pool.tensor_tensor(m.wl[:, a], m.raw[:, a], m.wh[:, a].bitcast(F32),
                                           ALU.subtract).then_inc(ws.w_split, 1)
            prefetch_split(pool, m, m.merge_ws, ws, 24)

        @block.tensor
        def _(pe):
            pe.sem_inc(*pe_did.credit())

            def gate(i, j, piece):
                a, g = piece // 3, piece % 3
                if g == 0:
                    pe.wait_ge(ws.w_split, 4 * i + (GATE0 + 2 * j + a + 3))
                before = (f"gate{piece - 3}_{j}", 0) if a else (f"gate{piece + 3}_{1 - j}", int(j == 0))
                pe.wait_ge(*act_did.at(before[0], i, before=before[1]))
                mm = three_pass(pe, gp[:, g, 0:GROUPS[g][1]], (lambda k: m.wh[:, a, k], lambda k: m.wl[:, a, k]),
                                (lambda k: m.hh[:, k], lambda k: m.hl[:, k]), GROUPS[g])
                mm.then_inc(*((ws.mm_done, 1) if g == 2 else pe_did.mark(f"gate{piece}_{j}")))

            pe.wait_ge(consts, 2)
            with pe.Fori(0, 2) as i:
                for j in J:
                    pe.wait_ge(ut_ld[j], 16 * i + 16)
                    pe.wait_ge(*dve_did.at(f"yt{1 - j}", i, before=int(j == 0)))
                    pe.sem_inc(m.pe_tick, 1)
                    frames = ut[:, j].rearrange("p (e t) -> p t e", t=C)
                    for s in range(C):
                        mm = pe.transpose(r4[0:NCH, s // 4, s % 4 * P:(s % 4 + 1) * P], frames[:, C - 1 - s], m.ident[:])
                    mm.then_inc(*pe_did.mark(f"uc{j}"))
                    gate(i, j, 0)
                    pe.wait_ge(*act_did.at(f"uc{j}", i))
                    pe.wait_ge(*dve_did.at(f"uc{j}", i))
                    pe.sem_inc(m.pe_tick, 1)
                    for n in range(2 * NB):
                        g, h = n // 2, n % 2
                        mm = pe.transpose(r4[:, n // 4, n % 4 * NCH:(n % 4 + 1) * NCH],
                                          uc[:, g, 8 * h:8 * h + 8], m.ident[0:NCH, 0:NCH])
                    mm.then_inc(*pe_did.mark(f"u2{j}"))
                    gate(i, j, 1)
                    pe.wait_ge(*act_did.at(f"u2{j}", i))
                    pe.wait_ge(*pool_did.at(f"w{j}", i))
                    pe.sem_inc(m.pe_tick, 1)
                    for n in range(2 * NB):
                        g, h = n // 2, n % 2
                        mm = pe.transpose(r4[:, n // 4, n % 4 * P:(n % 4 + 1) * P], w[:, g, 8 * h:8 * h + 8], m.ident[:])
                    mm.then_inc(*pe_did.mark(f"et{j}"))
                    gate(i, j, 2)
                    pe.wait_ge(*act_did.at(f"et{j}", i))
                    pe.wait_ge(*dve_did.at(f"et{j}", i))
                    pe.sem_inc(m.pe_tick, 1)
                    for g in range(NB):
                        mm = pe.matmul(r4[0:SC, g // 2, g % 2 * CS:(g % 2 + 1) * CS], tab[:, j, g, B1:B1 + SC],
                                       cl[:, g, 0:C], start=True, stop=True)
                    mm.then_inc(*pe_did.mark(f"k{j}"))
                    pe.wait_ge(*act_did.at(f"kp{j}", i))
                    pe.wait_ge(*dve_did.at(f"kp{j}", i))
                    pe.sem_inc(m.pe_tick, 1)
                    for g in range(NB):
                        for h in range(2):
                            mm = pe.matmul(r4[:, g // 4, g % 4 * NCH:(g % 4 + 1) * NCH], et[:, 2 * g + h, 0:P],
                                           u2[:, 2 * g + h], start=h == 0, stop=h == 1)
                    mm.then_inc(*pe_did.mark(f"v{j}"))
                    gate(i, j, 3)
                    pe.wait_ge(*act_did.at(f"vv{j}", i))
                    pe.sem_inc(m.pe_tick, 1)
                    for h in range(2):
                        mm = pe.matmul(r4[:, h, 0:NSW], swap[:], halves(vv)[:, h], start=True, stop=True)
                    mm.then_inc(*pe_did.mark(f"swap_v{j}"))
                    gate(i, j, 4)
                    pe.wait_ge(*dve_did.at(f"ww{j}", i))
                    pe.sem_inc(m.pe_tick, 1)
                    for h in range(2):
                        mm = pe.matmul(r4[:, h, 0:NSW], swap[:], halves(ww)[:, h], start=True, stop=True)
                    mm.then_inc(*pe_did.mark(f"swap_w{j}"))
                    gate(i, j, 5)
                    pe.wait_ge(*dve_did.at(f"sc{j}", i))
                    pe.wait_ge(tm_ld, 512 * i + 256 * (j + 1))
                    pe.sem_inc(m.pe_tick, 1)
                    for g in range(NB):
                        out = r4[0:NCH, g // 2, g % 2 * CS:(g % 2 + 1) * CS]
                        pe.matmul(out, u2[:, 2 * g + 1], tm1[:, g], start=True, stop=False)
                        pe.matmul(out[:, CS // 2:CS], u2[:, 2 * g], tm0[:, g], start=False, stop=False)
                        mm = pe.matmul(out, sc[:, g], cl[:, g, 1:C + 1], start=False, stop=True)
                    mm.then_inc(*pe_did.mark(f"y{j}"))
                    pe.wait_ge(*act_did.at(f"yc{j}", i))
                    pe.wait_ge(*dve_did.at(f"yc{j}", i))
                    pe.sem_inc(m.pe_tick, 1)
                    for t in range(C):
                        mm = pe.transpose(r4[:, t // 4, t % 4 * NCH:(t % 4 + 1) * NCH], yc[:, t], m.ident[0:NCH, 0:NCH])
                    mm.then_inc(*pe_did.mark(f"back{j}"))
            pe.wait_ge(*dve_did.at("yt1", 1))
            for n in range(2):
                mm = pe.transpose(r4[0:G32, n, 0:P], sf[:, :, n], m.ident[:])
            mm.then_inc(fin_mm, 1)

        @block.scalar
        def _(act):
            act.sem_inc(*act_did.credit())
            act.sem_inc(g_st, 16)
            act.sem_inc(y_st, 16)

            def gate(i, j, piece):
                a, g = piece // 3, piece % 3
                c0, cn = GROUPS[g]
                act.wait_ge(*((ws.mm_done, 4 * i + (GATE0 + 2 * j + a + 3)) if g == 2 else pe_did.at(f"gate{piece}_{j}", i)))
                if g == 0:
                    act.wait_ge(g_st, 64 * i + 16 * (2 * j + a + 1))
                act.activation(gout[:, c0:c0 + cn], gp[:, g, 0:cn], ACT.Tanh, scale=0.5).then_inc(
                    *act_did.mark(f"gate{piece}_{j}"))
                if g == 2:
                    act.wait_ge(*act_did.at(f"gate{piece}_{j}", i))
                    act.dma_start(m.gate_d[bass.ds((4 * i + (2 * j + a + GATE0)) * P, P), :], gout[:]).then_inc(g_st, 16)

            with act.Fori(0, 2) as i:
                for j in J:
                    act.wait_ge(*pe_did.at(f"uc{j}", i))
                    act.activation(*uc_bank(0), ACT.Copy)
                    act.activation(*uc_bank(1), ACT.Copy).then_inc(*act_did.mark(f"uc{j}"))
                    gate(i, j, 0)
                    act.wait_ge(*pe_did.at(f"u2{j}", i))
                    act.activation(u2[:].rearrange("p (b n) e -> p b (n e)", b=4), r4[:, :, 0:4 * NCH],
                                   ACT.Copy).then_inc(*act_did.mark(f"u2{j}"))
                    gate(i, j, 1)
                    act.wait_ge(*pe_did.at(f"et{j}", i))
                    act.wait_ge(*dve_did.at(f"cl{j}", i))
                    act.activation(et[:, 0:NB, 0:P], r4[:, 0:2].rearrange("p b (n c) -> p (b n) c", c=P),
                                   ACT.Copy).then_inc(*act_did.mark(f"et{j}"))
                    gate(i, j, 2)
                    act.wait_ge(*pe_did.at(f"k{j}", i))
                    act.activation(kp[:, 0:4, KW:], r4[0:SC, 0:2].rearrange("p b (g c) -> p (b g) c", c=CS),
                                   ACT.Copy).then_inc(*act_did.mark(f"kp{j}"))
                    act.wait_ge(*pe_did.at(f"v{j}", i))
                    act.activation(vv[:, :, NP_CH + 1:NP_CH + 2], tab[:, j, :, S0T:S0T + 1],
                                   ACT.Copy).then_inc(*act_did.mark(f"s0_{j}"))
                    v = r4[:, 0:2, 0:4 * NCH].rearrange("p b (g e) -> p b g e", e=NCH)
                    for b in range(2):
                        act.activation(vv[:, 4 * b:4 * b + 4, 1:NP_CH + 1], v[:, b, :, 0:NP_CH], ACT.Copy)
                        ins = act.activation(vv[:, 4 * b:4 * b + 4, NP_CH + 2:E70], v[:, b, :, NP_CH:NCH], ACT.Copy)
                    ins.then_inc(*act_did.mark(f"vv{j}"))
                    gate(i, j, 3)
                    gate(i, j, 4)
                    gate(i, j, 5)
                    act.wait_ge(*pe_did.at(f"y{j}", i))
                    for b in range(2):
                        ins = act.activation(yc.rearrange("e t (g c) -> e g t c", c=SC)[:, 2 * b:2 * b + 2],
                                             r4[0:NCH, b].rearrange("e (g t c) -> e g t c", g=2, c=SC), ACT.Copy)
                    ins.then_inc(*act_did.mark(f"yc{j}"))
                    act.wait_ge(*dve_did.at(f"yt{j}", i))
                    act.dma_start(m.ys_d[bass.ds((2 * i + j) * P, P), :], yt[:]).then_inc(y_st, 16)
            act.wait_ge(y_st, 80)
            act.wait_ge(g_st, 144)

        @block.vector
        def _(dve):
            dve.sem_inc(*dve_did.credit())
            for a in range(2):
                dve.tensor_copy(swap[:, a * SS:(a + 1) * SS], m.ident[:, (1 - a) * SS:(2 - a) * SS])
            dve.memset(kp[:, :, 0:KW], 0.0)
            dve.memset(vv[:, :, 0:1], 0.0)
            dve.memset(d0[:, :, NP_CH + 1:NP_CH + 2], 0.0)
            dve.memset(d0[:, :, 0:1], 0.0).then_inc(consts, 2)
            dve.wait_ge(consts, 2)
            with dve.Fori(0, 2) as i:
                for j in J:
                    at = lambda n: dve_did.at(f"{n}{j}", i)
                    mark = lambda n: dve_did.mark(f"{n}{j}")
                    dve.wait_ge(*pe_did.at(f"uc{j}", i))
                    dve.tensor_copy(*uc_bank(2))
                    dve.tensor_copy(*uc_bank(3)).then_inc(*mark("uc"))
                    dve.wait_ge(tab_ld[j], 16 * i + 16)
                    shape = [P, NB, C + 1, SC]
                    powers = lambda c: tab[:, j, :, c:c + C + 1].unsqueeze(3).to_broadcast(shape)
                    matrix = lambda c: tab[:, j, :, c:c + SC].unsqueeze(2).to_broadcast(shape)
                    tmp = et[:].rearrange("p n c -> p (n c)").rearrange("p (g k c) -> p g k c", g=NB, c=SC)
                    dve.tensor_tensor(cl[:], powers(PR), matrix(C1), ALU.mult).then_inc(*mark("cl_a"))
                    dve.tensor_tensor(tmp, powers(PI), matrix(C2), ALU.mult).then_inc(*mark("cl_b"))
                    dve.wait_ge(*at("cl_b"))
                    dve.tensor_tensor(cl[:], cl[:], tmp, ALU.add).then_inc(*mark("cl"))
                    dve.wait_ge(*at("cl"))
                    dve.wait_ge(*pe_did.at(f"et{j}", i))
                    dve.tensor_copy(et[:, NB:, 0:P], r4[:, 2:4].rearrange("p b (n c) -> p (b n) c", c=P)
                                    ).then_inc(*mark("et"))
                    r16 = tab[:, j, :, R16:R16 + 1]
                    dve.tensor_copy(d0[:, :, 1:NP_CH + 1], r16.to_broadcast([P, NB, NP_CH]))
                    dve.tensor_copy(d0[:, :, NP_CH + 2:E70], r16.to_broadcast([P, NB, NS_CH])).then_inc(*mark("d0"))
                    dve.wait_ge(*pe_did.at(f"k{j}", i))
                    dve.tensor_copy(kp[:, 4:8, KW:], r4[0:SC, 2:4].rearrange("p b (g c) -> p (b g) c", c=CS)
                                    ).then_inc(*mark("kp"))
                    rc, rs = tab[:, j, :, RC:RC + E70], tab[:, j, :, RS:RS + E70]
                    sw = lambda b: r4[:, b, 0:NSW].rearrange("p (g e) -> p g e", e=E70)
                    dve.wait_ge(*act_did.at(f"vv{j}", i))
                    dve.tensor_tensor(x1[:], vv[:], rc, ALU.mult).then_inc(*mark("x1"))
                    dve.wait_ge(*pe_did.at(f"swap_v{j}", i))
                    for b in range(2):
                        ins = dve.tensor_tensor(x2[:, 4 * b:4 * b + 4], sw(b), rs[:, 4 * b:4 * b + 4], ALU.mult)
                    ins.then_inc(*mark("x2"))
                    dve.wait_ge(*at("x2"))
                    dve.tensor_tensor(x1[:], x1[:], x2[:], ALU.subtract).then_inc(*mark("d1"))
                    dve.wait_ge(*at("d1"))
                    dve.tensor_tensor_scan(flat(ww), flat(d0), flat(x1), 0.0, ALU.mult, ALU.add).then_inc(*mark("ww"))
                    dve.wait_ge(*at("ww"))
                    dve.tensor_tensor(x1[:], ww[:], rc, ALU.mult).then_inc(*mark("x3"))
                    dve.wait_ge(*pe_did.at(f"swap_w{j}", i))
                    for b in range(2):
                        ins = dve.tensor_tensor(vv[:, 4 * b:4 * b + 4], sw(b), rs[:, 4 * b:4 * b + 4], ALU.mult)
                    ins.then_inc(*mark("x4"))
                    dve.wait_ge(*at("x4"))
                    dve.tensor_tensor(sf[:, bass.ds((2 * i + j) * NB, NB)], x1[:, :, NP_CH:E70:NS_CH + 1],
                                      vv[:, :, NP_CH:E70:NS_CH + 1], ALU.add).then_inc(*mark("sf"))
                    dve.tensor_tensor(sc[:, :, 0:NP_CH], x1[:, :, 0:NP_CH], vv[:, :, 0:NP_CH], ALU.add)
                    dve.tensor_tensor(sc[:, :, NP_CH:NCH], x1[:, :, NP_CH + 1:E70 - 1], vv[:, :, NP_CH + 1:E70 - 1],
                                      ALU.add).then_inc(*mark("sc"))
                    dve.wait_ge(*pe_did.at(f"y{j}", i))
                    for b in (2, 3):
                        ins = dve.tensor_copy(yc.rearrange("e t (g c) -> e g t c", c=SC)[:, 2 * b:2 * b + 2],
                                              r4[0:NCH, b].rearrange("e (g t c) -> e g t c", g=2, c=SC))
                    ins.then_inc(*mark("yc"))
                    dve.wait_ge(*pe_did.at(f"back{j}", i))
                    dve.wait_ge(y_st, 32 * i + 16 * (j + 1))
                    for b in range(4):
                        t = slice(4 * b, 4 * b + 4)
                        ins = dve.scalar_tensor_tensor(
                            out=yt[:].rearrange("p (e t) -> p t e", t=C)[:, t],
                            in0=ut[:, j].rearrange("p (e t) -> p t e", t=C)[:, t],
                            scalar=m.vec[:, bass.ds(28 + 2 * i + j, 1)],
                            in1=r4[:, b, 0:4 * NCH].rearrange("p (t e) -> p t e", e=NCH), op0=ALU.mult, op1=ALU.add)
                    ins.then_inc(*mark("yt"))
            dve.wait_ge(fin_mm, 1)
            dve.tensor_copy(fin, r4[0:G32, 0:2, 0:P]).then_inc(fin_out, 1)



def stage_merge(nc, m, io):
    with ExitStack() as ctx:
        sb = lambda n, s, d=F32: ctx.enter_context(nc.sbuf_tensor(n, s, d))
        ps = lambda n, s: ctx.enter_context(nc.psum_tensor(n, s, F32))
        sem = StageSems(nc)
        ctx.callback(sem.close)
        ORDER = (0, 2, 1)
        acc = [ps(f"mg_ps{a}", [P, 3, 512]) for a in range(2)]
        merged, prod, gate = sb("merged", [P, KD * T]), sb("prod", [P, T]), sb("gate", [P, 2, T])
        y, sig = sb("y", [P, MW, T]), sb("sig", [P, 2, T])
        yh, yl = sb("y_hi", [P, MW, T], F32R), sb("y_lo", [P, MW, T], F32R)
        branch = {0: (m.hh[:, 0:MW], m.hl[:, 0:MW]), 2: (m.hh[:, MW:KD], m.hl[:, MW:KD]), 1: (yh[:], yl[:])}
        hh, hl = (t[:].rearrange("p k t -> p (k t)") for t in (m.hh, m.hl))
        ws = m.merge_ws
        y_ld = [sem(f"y_ld{k}") for k in range(MW)]
        b2_ld, g_ld = sem("b2_ld"), [sem("g_ld0"), sem("g_ld1")]
        even_mm, prod_done, sum_done, hi, lo = (sem(n) for n in ("even_mm", "prod_done", "sum_done", "hi", "lo"))
        tiles = range(MW)
        act_did = Steps(sem("act_did"), [f"{n}{k}" for k in tiles for n in ("gelu", "y_hi")] + [f"sig{o}" for o in tiles] +
                        [f"r_hi{o}" for o in tiles])
        dve_did = Steps(sem("dve_did"), [f"y_lo{k}" for k in tiles] + [f"r{o}" for o in tiles] + [f"r_lo{o}" for o in tiles])
        block = ctx.enter_context(nc.Block())

        def pair(ph, i):
            return i + (4 * ph + (2 if ph else 0))

        @block.sync
        def _(sp):
            for ph, n in enumerate(ORDER):
                with sp.Fori(int(ph == 0), 2) as i:
                    for a in range(2):
                        sp.wait_ge(ws.w_split, 2 * i + (pair(ph, 0) + a + 1))
                        sp.dma_start(two_tiles(m.raw[:, a]),
                                     column_blocks(io["w_branch"][0, n], MW)[:, :, bass.ds((2 * i + a) * 2 * P, 2 * P)]
                                     ).then_inc(ws.raw_ld[a], 16)
                if ph == 0:
                    for a in range(2):
                        sp.wait_ge(ws.w_split, 4 + a + 1)
                        sp.dma_start(two_tiles(m.raw[:, a]),
                                     column_blocks(io["w_glu"][0], MW)[:, :, 2 * a * P:2 * (a + 1) * P]).then_inc(ws.raw_ld[a], 16)
            w_out = column_blocks(io["w_out"][0], KD)
            prefetch_blocks(sp, m, m.out_ws, [(w_out[:, :, a * P:(a + 1) * P], whole) for a in range(2)], ws, 14)

        @block.gpsimd
        def _(pool):
            split_weights(pool, 7, m, ws, first=1)
            prefetch_split(pool, m, m.out_ws, ws, 14)

        @block.tensor
        def _(pe):
            pe.sem_inc(ws.mm_done, 2)

            def tile(a, c, rhs, k_ready=None):
                for k in tiles:
                    if k_ready:
                        pe.wait_ge(*k_ready(k))
                    for g, cols in enumerate(GROUPS):
                        mm = three_pass(pe, acc[c][:, g, 0:cols[1]],
                                        (lambda k: m.wh[:, a, 2 * k + c], lambda k: m.wl[:, a, 2 * k + c]),
                                        (lambda k: rhs[0][:, k], lambda k: rhs[1][:, k]), cols, first=k == 0,
                                        last=k == MW - 1, ks=[k])
                mm.then_inc(ws.mm_done if c else even_mm, 1)

            for ph, n in enumerate(ORDER):
                if ph == 1:
                    pe.wait_ge(b2_ld, 32)
                    pe.wait_ge(*act_did.at("sig3"))
                elif ph == 2:
                    pe.wait_ge(*dve_did.at("r_lo3"))
                else:
                    pe.wait_ge(m.b0_ld, 32)
                with pe.Fori(0, 2) as i:
                    for a in range(2):
                        pe.wait_ge(ws.w_split, 2 * i + (pair(ph, 0) + a + 3))
                        for c in range(2):
                            pe.wait_ge(prod_done, 4 * i + (8 * ph + 2 * a + c + 1))
                            tile(a, c, branch[n])
                if ph == 0:
                    for o in tiles:
                        pe.wait_ge(ws.w_split, 4 + o // 2 + 3)
                        if o < 2:
                            pe.wait_ge(prod_done, 9 + o)
                        else:
                            pe.wait_ge(*act_did.at(f"sig{o - 2}"))
                        tile(o // 2, o % 2, (yh[:], yl[:]), (lambda k: dve_did.at(f"y_lo{k}")) if o == 0 else None)

        @block.scalar
        def _(act):
            def gates(ph, i, c):
                act.wait_ge(prod_done, 2 * i + (8 * ph + c + 1))
                act.dma_start(gate[:, c], m.gate_d[bass.ds((2 * i + (8 * ORDER[ph] + c)) * P, P), :]).then_inc(g_ld[c], 16)

            for p in range(4):
                gates(0, p, 0)
                gates(0, p, 1)
                if p == 0:
                    for k in tiles:
                        act.dma_start(y[:, k], m.ys_d[k * P:(k + 1) * P]).then_inc(y_ld[k], 16)
                    for src, dst in zip((m.yh_d, m.yl_d), branch[2]):
                        act.dma_start(dst.bitcast(F32), src[2].rearrange("(k p) t -> p k t", p=P)).then_inc(b2_ld, 16)
                act.wait_ge(y_ld[p], 16)
                act.activation(y[:, p], y[:, p], ACT.Gelu_apprx_tanh).then_inc(*act_did.mark(f"gelu{p}"))
                act.wait_ge(*act_did.at(f"gelu{p}"))
                act.activation(yh[:, p], y[:, p], ACT.Copy).then_inc(*act_did.mark(f"y_hi{p}"))
            gates(1, 0, 0)
            gates(1, 0, 1)
            for o in tiles:
                act.wait_ge(*((ws.mm_done, 4 + o // 2 + 3) if o % 2 else (even_mm, 4 + o // 2 + 1)))
                if o >= 2:
                    act.wait_ge(*dve_did.at(f"r{o - 2}"))
                for g, (c0, cn) in enumerate(GROUPS):
                    ins = act.activation(sig[:, o % 2, c0:c0 + cn], acc[o % 2][:, g, 0:cn], ACT.Sigmoid,
                                         bias=m.vec[:, 32 + o:33 + o])
                ins.then_inc(*act_did.mark(f"sig{o}"))
            for o in tiles:
                act.wait_ge(*dve_did.at(f"r{o}"))
                act.activation(yh[:, o], y[:, o], ACT.Copy).then_inc(*act_did.mark(f"r_hi{o}"))
            for ph in (1, 2):
                with act.Fori(int(ph == 1), 4) as i:
                    gates(ph, i, 0)
                    gates(ph, i, 1)
                    if ph == 2:
                        for c in range(2):
                            act.wait_ge(sum_done, 2 * i + (17 + c))
                            act.activation(hh[:, bass.ds((2 * i + c) * T, T)], merged[:, bass.ds((2 * i + c) * T, T)],
                                           ACT.Copy, scale=0.5).then_inc(hi, 1)

        @block.vector
        def _(dve):
            dve.sem_inc(prod_done, 2)

            def gated(ph, i, c):
                d, at = 2 * i + c, 2 * i + (8 * ph + c)
                dve.wait_ge(g_ld[c], 16 * i + 16 * (4 * ph + 1))
                dve.wait_ge(*((ws.mm_done, pair(ph, i) + 3) if c else (even_mm, pair(ph, i) + 1)))
                if ph:
                    dve.wait_ge(sum_done, at)
                for g, (c0, cn) in enumerate(GROUPS):
                    dst = prod[:, c0:c0 + cn] if ph else merged[:, bass.ds(d * T + c0, cn)]
                    ins = dve.scalar_tensor_tensor(out=dst, in0=gate[:, c, c0:c0 + cn], scalar=1.0,
                                                   in1=acc[c][:, g, 0:cn], op0=ALU.add, op1=ALU.mult)
                ins.then_inc(prod_done, 1)
                dve.wait_ge(prod_done, at + 3)
                if ph == 0:
                    dve.sem_inc(sum_done, 1)
                else:
                    dve.tensor_tensor(merged[:, bass.ds(d * T, T)], merged[:, bass.ds(d * T, T)], prod[:],
                                      ALU.add).then_inc(sum_done, 1)

            for p in range(4):
                gated(0, p, 0)
                gated(0, p, 1)
                dve.wait_ge(*act_did.at(f"y_hi{p}"))
                dve.tensor_tensor(yl[:, p], y[:, p], yh[:, p].bitcast(F32), ALU.subtract).then_inc(*dve_did.mark(f"y_lo{p}"))
            dve.wait_ge(*dve_did.at("y_lo3"))
            for o in tiles:
                dve.wait_ge(*act_did.at(f"sig{o}"))
                dve.tensor_tensor(y[:, o], sig[:, o % 2], y[:, o], ALU.mult).then_inc(*dve_did.mark(f"r{o}"))
            dve.wait_ge(ws.mm_done, 8)
            for o in tiles:
                dve.wait_ge(*act_did.at(f"r_hi{o}"))
                dve.wait_ge(*dve_did.at(f"r{o}"))
                dve.tensor_tensor(yl[:, o], y[:, o], yh[:, o].bitcast(F32), ALU.subtract).then_inc(*dve_did.mark(f"r_lo{o}"))
            for ph in (1, 2):
                with dve.Fori(0, 4) as i:
                    for c in range(2):
                        gated(ph, i, c)
                    if ph == 2:
                        for c in range(2):
                            d = 2 * i + c
                            dve.wait_ge(hi, 2 * i + (c + 1))
                            dve.scalar_tensor_tensor(out=hl[:, bass.ds(d * T, T)], in0=merged[:, bass.ds(d * T, T)],
                                                     scalar=0.5, in1=hh[:, bass.ds(d * T, T)].bitcast(F32),
                                                     op0=ALU.mult, op1=ALU.subtract).then_inc(lo, 1)



def stage_out(nc, m, io):
    with ExitStack() as ctx:
        sb = lambda n, s, d=F32: ctx.enter_context(nc.sbuf_tensor(n, s, d))
        ps = lambda n, s: ctx.enter_context(nc.psum_tensor(n, s, F32))
        sem = StageSems(nc)
        ctx.callback(sem.close)
        NPASS = NF // 2
        HP, HS = 2, TP + 4
        UP = HS + TS
        up, cv = sb("up_raw", [P, 2, UP]), sb("conv", [P, 2, UP - 2])
        s_, ah, al = sb("ffn_act", [P, T]), sb("ffn_hi", [P, 2, T], F32R), sb("ffn_lo", [P, 2, T], F32R)
        dwh, dwl = sb("down_hi", [P, 2, 8, P], F32R), sb("down_lo", [P, 2, 8, P], F32R)
        last, last_t = sb("last", [P, 2, 88]), sb("last_t", [88, 2, P])
        acc = [ps(f"ffn_ps{a}", [P, 3, 512]) for a in range(2)]
        m.xt, inv = sb("xt", [P, KD, T]), sb("n2_inv", [P, T])
        ow, x_ld, x_sum, acc_zero = m.out_ws, sem("x_ld"), sem("x_sum"), sem("acc_zero")
        b2, s2 = NormBuffers(up[:, :, 0:T], s_, inv, cv[:, :, 0:T], acc[0]), NormSems(sem, "n2")
        xt, w_out = m.xt[:].rearrange("p k t -> p (k t)"), column_blocks(io["w_out"][0], KD)
        tps = ps("last_ps", [P, 512])
        raw_ld, zeroed, last_turned, last_out, st, final_mm, final_add = (
            [sem("ffn_raw_ld0"), sem("ffn_raw_ld1")], sem("zeroed"), sem("last_turned"), sem("last_out"), sem("conv_st"),
            sem("final_mm"), sem("final_add"))
        b, s = NormBuffers(up, s_, cv[:, 0], None, acc[0]), NormSems(sem, "n3")
        turned, y_out, y_st = sem("turned"), [sem("y_out0"), sem("y_out1")], [sem("y_st0"), sem("y_st1")]
        y = m.raw[:].rearrange("p a k c -> p a (k c)")
        halves = ("g", "v")
        blocks = ("g0", "v0", "down0", "down1", "g1", "v1")
        pool_did = Steps(sem("pool_did"), [f"{n}{b}" for b in blocks for n in ("hi_", "lo_")], loop=True)
        pe_did = Steps(sem("pe_did"), ["g0", "v0"] + [f"down{d}" for d in range(KD)] + ["g1", "v1"], loop=True)
        act_did = Steps(sem("act_did"), [n for j in range(2) for n in
                        [f"{x}_{h}{j}" for h in halves for x in ("hist", "raw", "save", "base")] +
                        [f"silu{j}", f"hi{j}"]], loop=True)
        dve_did = Steps(sem("dve_did"), [f"tap{t}_g0" for t in (1, 0)] + ["add0"] + [f"tap{t}_v0" for t in (1, 0)] +
                        ["add1", "add2", "s0"] + [f"add{d}" for d in range(3, KD)] + ["lo0"] +
                        [f"tap{t}_{h}1" for h in halves for t in (1, 0)] + ["s1", "lo1"], loop=True)
        w_up, w_down = column_blocks(io["w_up"][0], KD), io["w_down"][0]
        by_tile = lambda t, n: t.rearrange("p (r f) -> p f r", r=n)
        block = ctx.enter_context(nc.Block())

        def tile_of(i, h, j):
            return 2 * i + (j + (NF if h == "v" else 0))

        @block.sync
        def _(sp):
            with sp.Fori(1, 4) as i:
                for a in range(2):
                    sp.wait_ge(ow.w_split, 2 * i + (a + 1))
                    sp.dma_start(m.raw[:, a], w_out[:, :, bass.ds((2 * i + a) * P, P)]).then_inc(ow.raw_ld[a], 16)
            sp.wait_ge(ow.w_split, 10)

            def load(i, n, blk):
                sp.wait_ge(*pool_did.at(f"lo_{blocks[n - 2]}", i, before=int(n < 2)))
                if blk[0] == "d":
                    src = w_down[bass.ds((2 * i + (int(blk[-1]) - 2)) * P, P), :].rearrange("p (d c) -> p d c", c=P)
                else:
                    src = w_up[:, :, bass.ds(tile_of(i, blk[0], int(blk[1])) * P, P)]
                sp.dma_start(m.raw[:, n % 2], src).then_inc(raw_ld[n % 2], 16)

            def one_pass(i, downs):
                for n, blk in enumerate(blocks):
                    if downs or blk[0] != "d":
                        load(i, n, blk)

            for a in range(2):
                sp.sem_inc(raw_ld[a], 16)
            one_pass(0, False)
            with sp.Fori(1, NPASS) as i:
                one_pass(i, True)
            for a in range(2):
                sp.wait_ge(*pool_did.at(f"lo_{blocks[4 + a]}", NPASS - 1))
                sp.dma_start(m.raw[:, a], w_down[(NF - 2 + a) * P:(NF - 1 + a) * P].rearrange("p (d c) -> p d c", c=P)
                             ).then_inc(raw_ld[a], 16)
            sp.wait_ge(last_out, 1)
            for n, dst in enumerate((io["conv_p"], io["conv_s"])):
                sp.dma_start(dst[0, 0].rearrange("r (f c) -> (r f) c", c=P), last_t[:, n]).then_inc(st, 16)
            for j, (c0, cn) in enumerate(TOK):
                a = j % 2
                sp.wait_ge(y_out[a], j // 2 + 1)
                dst = io["y_prompt"][0, c0:c0 + cn] if j < 8 else io["y_sample"][0]
                sp.dma_start(dst, y[0:cn, a]).then_inc(y_st[a], 16)
            sp.wait_ge(y_st[0], 80)
            sp.wait_ge(y_st[1], 64)
            sp.wait_ge(st, 32)

        @block.gpsimd
        def _(pool):
            pool.sem_inc(*pool_did.credit())
            split_weights(pool, 4, m, ow, first=1)
            pool.wait_ge(ow.mm_done, 10)

            def split(i, n, blk, ld):
                hi, lo = (dwh, dwl) if blk[0] == "d" else (m.wh, m.wl)
                a = n % 2
                pool.wait_ge(raw_ld[a], ld)
                if blk[0] == "d":
                    pool.wait_ge(*pe_did.at(f"down{KD - 1}", i, before=1))
                else:
                    other = blk[0] + str(1 - int(blk[1]))
                    pool.wait_ge(*pe_did.at(other, i, before=int(blk[1] == "0")))
                pool.sem_inc(m.pool_tick, 1)
                pool.tensor_copy(hi[:, a], m.raw[:, a]).then_inc(*pool_did.mark(f"hi_{blk}"))
                pool.wait_ge(*pool_did.at(f"hi_{blk}", i))
                pool.tensor_tensor(lo[:, a], m.raw[:, a], hi[:, a].bitcast(F32),
                                   ALU.subtract).then_inc(*pool_did.mark(f"lo_{blk}"))

            def one_pass(i, downs):
                for n, blk in enumerate(blocks):
                    if blk[0] == "d" and not downs:
                        pool.wait_ge(*pool_did.at("lo_v0"))
                        pool.sem_inc(*pool_did.mark(f"hi_{blk}"))
                        pool.sem_inc(*pool_did.mark(f"lo_{blk}"))
                    else:
                        split(i, n, blk, 48 * i + 16 * (n // 2 + 1) if downs else (32, 48)[n // 4])

            one_pass(0, False)
            with pool.Fori(1, NPASS) as i:
                one_pass(i, True)
            pool.wait_ge(*pool_did.at("lo_v1", NPASS - 1))
            for blk, n in (("g0", 0), ("v0", 1)):
                pool.sem_inc(*pool_did.mark(f"hi_{blk}"))
                pool.sem_inc(*pool_did.mark(f"lo_{blk}"))
            for n in (2, 3):
                split(NPASS, n, blocks[n], 48 * NPASS + 16)

        @block.tensor
        def _(pe):
            pe.sem_inc(ow.mm_done, 2)
            pe.sem_inc(*pe_did.credit())
            with pe.Fori(0, 4) as i:
                for a in range(2):
                    pe.wait_ge(ow.w_split, 2 * i + (a + 3))
                    pe.wait_ge(x_sum, 2 * i + (a + 1))
                    for g, cols in enumerate(GROUPS):
                        mm = three_pass(pe, acc[a][:, g, 0:cols[1]], (lambda k: m.wh[:, a, k], lambda k: m.wl[:, a, k]),
                                        (lambda k: m.hh[:, k], lambda k: m.hl[:, k]), cols)
                    mm.then_inc(ow.mm_done, 1)
            norm_tensor(pe, m, b2, s2, squares=KD)
            pe.wait_ge(s2.root_done, len(GROUPS))

            def up_tile(i, h, j, k_ready=None, first=False):
                a = halves.index(h)
                pe.wait_ge(*pool_did.at(f"lo_{h}{j}", i))
                if j == 0:
                    pe.wait_ge(*act_did.at(f"raw_{h}1", i, before=1))
                elif first:
                    pe.wait_ge(*act_did.at(f"raw_{h}0", i))
                else:
                    pe.wait_ge(*dve_did.at(f"add{KD - 2 + a}", i))
                if k_ready is not None:
                    for k in range(KD):
                        pe.wait_ge(k_ready, k + 1)
                        for g, cols in enumerate(GROUPS):
                            mm = three_pass(pe, acc[a][:, g, 0:cols[1]],
                                            (lambda k: m.wh[:, a, k], lambda k: m.wl[:, a, k]),
                                            (lambda k: m.hh[:, k], lambda k: m.hl[:, k]), cols, first=k == 0,
                                            last=k == KD - 1, ks=[k])
                else:
                    for g, cols in enumerate(GROUPS):
                        mm = three_pass(pe, acc[a][:, g, 0:cols[1]],
                                        (lambda k: m.wh[:, a, k], lambda k: m.wl[:, a, k]),
                                        (lambda k: m.hh[:, k], lambda k: m.hl[:, k]), cols)
                mm.then_inc(*pe_did.mark(f"{h}{j}"))

            def downs(i, final=False):
                pe.wait_ge(*pool_did.at("lo_down1", i))
                pe.wait_ge(*dve_did.at("lo1", i, before=1))
                for d in range(KD):
                    a = d % 2
                    if d >= 2:
                        pe.wait_ge(*((final_add, d - 1) if final else dve_did.at(f"add{d - 2}", i)))
                    else:
                        pe.wait_ge(*act_did.at(f"raw_{halves[a]}{int(final)}", i, before=int(final)))
                    for g, cols in enumerate(GROUPS):
                        mm = three_pass(pe, acc[a][:, g, 0:cols[1]], (lambda k: dwh[:, k, d], lambda k: dwl[:, k, d]),
                                        (lambda k: ah[:, k], lambda k: al[:, k]), cols, ks=range(2))
                    mm.then_inc(*((final_mm, 1) if final else pe_did.mark(f"down{d}")))

            def one_pass(i, first=False):
                up_tile(i, "g", 0, s2.lo_ready if first else None)
                up_tile(i, "v", 0)
                if first:
                    pe.wait_ge(*pe_did.at("v0"))
                    for d in range(KD):
                        pe.sem_inc(*pe_did.mark(f"down{d}"))
                else:
                    downs(i)
                up_tile(i, "g", 1, first=first)
                up_tile(i, "v", 1, first=first)

            one_pass(0, first=True)
            with pe.Fori(1, NPASS) as i:
                one_pass(i)
            pe.wait_ge(*act_did.at("save_v1", NPASS - 1))
            for n in range(2):
                mm = pe.transpose(tps[0:88, n * P:(n + 1) * P], last[:, n], m.ident[:])
            mm.then_inc(last_turned, 1)
            downs(NPASS, final=True)
            norm_tensor(pe, m, b, s, squares=KD)
            for j, (c0, cn) in enumerate(TOK):
                a = j % 2
                if j in (0, 4):
                    pe.wait_ge(s.nt_ready, KD * (1 + j // 4))
                if j >= 2:
                    pe.wait_ge(y_out[a], j // 2)
                for k in range(KD):
                    mm = pe.transpose(acc[a][0:cn, k // 4, k % 4 * P:(k % 4 + 1) * P], m.xt[:, k, c0:c0 + cn], m.ident[:])
                mm.then_inc(turned, 1)

        def frames_out(j, copy, wait):
            a, cn = j % 2, TOK[j][1]
            wait(turned, j + 1)
            if j >= 2:
                wait(y_st[a], 16 * (j // 2))
            copy(y[0:cn, a], acc[a][0:cn, 0:2].rearrange("p b c -> p (b c)")).then_inc(y_out[a], 1)

        @block.scalar
        def _(act):
            act.dma_start(m.xt[:], m.xt_d).then_inc(x_ld, 16)
            act.sem_inc(s2.sq_ready, 1)
            act.sem_inc(*act_did.credit())
            with act.Fori(0, 4) as i:
                for a in range(2):
                    act.wait_ge(x_sum, 2 * i + (a + 3))
                    act.activation(b2.sq[:, a], xt[:, bass.ds((2 * i + a) * T, T)], ACT.Square).then_inc(s2.sq_ready, 1)
            norm_scalar(act, m, b2, s2, squares=False)

            def half(i, h, j):
                a, f = halves.index(h), tile_of(i, h, j)
                act.wait_ge(*pe_did.at(f"{h}{j}", i))
                act.wait_ge(*dve_did.at(f"tap0_{h}{1 - j}", i, before=int(j == 0)))
                act.activation(up[:, a, TP + 2:TP + 4].unsqueeze(1), by_tile(m.chist[:], 2)[:, bass.ds(f, 1)],
                               ACT.Copy).then_inc(*act_did.mark(f"hist_{h}{j}"))
                for g, (c0, cn) in enumerate(GROUPS):
                    n = min(TP - c0, cn)
                    ins = act.activation(up[:, a, HP + c0:HP + c0 + n], acc[a][:, g, 0:n], ACT.Copy)
                ins = act.activation(up[:, a, HS:UP], acc[a][:, 2, n:cn], ACT.Copy)
                ins.then_inc(*act_did.mark(f"raw_{h}{j}"))
                act.wait_ge(*act_did.at(f"raw_{h}{j}", i))
                for n, c0 in enumerate((TP, UP - 2)):
                    ins = act.activation(by_tile(last[:, n], 2)[:, bass.ds(f, 1)], up[:, a, c0:c0 + 2].unsqueeze(1), ACT.Copy)
                ins.then_inc(*act_did.mark(f"save_{h}{j}"))
                act.wait_ge(*dve_did.at(f"s{1 - j}", i, before=int(j == 0)))
                act.activation(cv[:, a], up[:, a, 2:UP], ACT.Identity, scale=m.cw2[:, bass.ds(f, 1)],
                               bias=m.vec[:, bass.ds(f + 36, 1)]).then_inc(*act_did.mark(f"base_{h}{j}"))

            def one_pass(i):
                for j in range(2):
                    half(i, "g", j)
                    half(i, "v", j)
                    act.wait_ge(*dve_did.at(f"tap0_g{j}", i))
                    act.activation(cv[:, 0], cv[:, 0], ACT.Silu).then_inc(*act_did.mark(f"silu{j}"))
                    act.wait_ge(*dve_did.at(f"s{j}", i))
                    if j == 0:
                        act.wait_ge(*pe_did.at(f"down{KD - 1}", i))
                    act.activation(ah[:, j], s_[:], ACT.Copy).then_inc(*act_did.mark(f"hi{j}"))

            one_pass(0)
            with act.Fori(1, NPASS) as i:
                one_pass(i)
            for d in range(KD):
                act.wait_ge(final_add, d + 1)
                if d >= 2:
                    act.wait_ge(s.sq_used, d - 1)
                act.activation(b.sq[:, d % 2, 0:T], m.xt[:, d], ACT.Square).then_inc(s.sq_ready, 1)
            norm_scalar(act, m, b, s, split=False, squares=False)
            for j in range(0, 9, 2):
                frames_out(j, lambda o, i: act.activation(o, i, ACT.Copy), act.wait_ge)

        @block.vector
        def _(dve):
            dve.sem_inc(x_sum, 2)
            dve.sem_inc(*dve_did.credit())
            dve.memset(s_[:], 0.0).then_inc(acc_zero, 1)
            dve.wait_ge(acc_zero, 1)
            dve.wait_ge(x_ld, 16)
            with dve.Fori(0, 4) as i:
                for a in range(2):
                    dve.wait_ge(ow.mm_done, 2 * i + (a + 3))
                    for g, (c0, cn) in enumerate(GROUPS):
                        x = xt[:, bass.ds((2 * i + a) * T + c0, cn)]
                        ins = dve.tensor_tensor(x, acc[a][:, g, 0:cn], x, ALU.add)
                    ins.then_inc(x_sum, 1)
                for a in range(2):
                    dve.wait_ge(s2.sq_ready, 2 * i + (a + 2))
                    if a:
                        dve.wait_ge(s2.sq_used, 2 * i + 1)
                    dve.tensor_tensor(s_[:], s_[:], b2.sq[:, a], ALU.add).then_inc(s2.sq_used, 1)
                dve.wait_ge(s2.sq_used, 2 * i + 2)
            norm_vector(dve, m, b2, s2, m.vec[:, 8:16], squares=False)
            dve.wait_ge(s2.lo_ready, KD)
            for a in range(2):
                ins = dve.memset(up[:, a, 0:HP], 0.0)
            ins.then_inc(zeroed, 1)
            dve.wait_ge(zeroed, 1)

            def taps(i, h, j):
                a, f = halves.index(h), tile_of(i, h, j)
                for t in (1, 0):
                    dve.wait_ge(*(act_did.at(f"base_{h}{j}", i) if t else dve_did.at(f"tap1_{h}{j}", i)))
                    dve.scalar_tensor_tensor(out=cv[:, a], in0=up[:, a, t:UP - 2 + t],
                                             scalar=m.cw01[:, bass.ds(f + 44 * t, 1)], in1=cv[:, a], op0=ALU.mult,
                                             op1=ALU.add).then_inc(*dve_did.mark(f"tap{t}_{h}{j}"))

            def gated(i, j):
                dve.wait_ge(*act_did.at(f"silu{j}", i))
                dve.wait_ge(*dve_did.at(f"tap0_v{j}", i))
                for c0, v0, cn in ((0, 0, TP), (TP, HS - 2, TS)):
                    ins = dve.tensor_tensor(s_[:, c0:c0 + cn], cv[:, 0, v0:v0 + cn], cv[:, 1, v0:v0 + cn], ALU.mult)
                ins.then_inc(*dve_did.mark(f"s{j}"))

            def low(i, j):
                dve.wait_ge(*act_did.at(f"hi{j}", i))
                dve.wait_ge(*dve_did.at(f"s{j}", i))
                dve.tensor_tensor(al[:, j], s_[:], ah[:, j].bitcast(F32), ALU.subtract).then_inc(*dve_did.mark(f"lo{j}"))

            def add(i, d, first=False, final=False):
                if first:
                    dve.wait_ge(*dve_did.at({0: "tap0_g0", 1: "tap0_v0", 2: "tap0_v0"}.get(d, "s0")))
                    dve.sem_inc(*dve_did.mark(f"add{d}"))
                    return
                dve.wait_ge(*((final_mm, d + 1) if final else pe_did.at(f"down{d}", i)))
                for g, (c0, cn) in enumerate(GROUPS):
                    ins = dve.tensor_tensor(m.xt[:, d, c0:c0 + cn], acc[d % 2][:, g, 0:cn], m.xt[:, d, c0:c0 + cn], ALU.add)
                ins.then_inc(*((final_add, 1) if final else dve_did.mark(f"add{d}")))

            def one_pass(i, first=False):
                taps(i, "g", 0)
                add(i, 0, first)
                taps(i, "v", 0)
                add(i, 1, first)
                add(i, 2, first)
                gated(i, 0)
                for d in range(3, KD):
                    add(i, d, first)
                low(i, 0)
                taps(i, "g", 1)
                taps(i, "v", 1)
                gated(i, 1)
                low(i, 1)

            one_pass(0, first=True)
            with dve.Fori(1, NPASS) as i:
                one_pass(i)
            dve.wait_ge(last_turned, 1)
            dve.tensor_copy(last_t[:].rearrange("p n c -> p (n c)"), tps[0:88, 0:2 * P]).then_inc(last_out, 1)
            dve.wait_ge(*dve_did.at("lo1", NPASS - 1))
            dve.memset(s_[:], 0.0).then_inc(zeroed, 1)
            dve.wait_ge(zeroed, 2)

            def add_square(d):
                dve.wait_ge(s.sq_ready, d + 1)
                if d:
                    dve.wait_ge(s.sq_used, d)
                dve.tensor_tensor(s_[:], s_[:], b.sq[:, d % 2, 0:T], ALU.add).then_inc(s.sq_used, 1)

            for d in range(KD):
                add(NPASS, d, final=True)
                if d:
                    add_square(d - 1)
            add_square(KD - 1)
            norm_vector(dve, m, b, s, m.vec[:, 16:24], split=False, squares=False)
            for j in range(1, 9, 2):
                frames_out(j, dve.tensor_copy, dve.wait_ge)



STAGES = (stage_input, stage_project, stage_small, stage_attention, stage_ssm, stage_merge, stage_out)



INPUTS = ["x_prompt", "x_sample", "cache_pool", "state_ssm_re", "state_ssm_im", "cache_k", "cache_v", "cache_logf",
          "cache_ffn_conv", "norm_mix_g", "w_in", "b_f", "w_pool", "pool_scale", "lam_re", "lam_im", "log_dt", "b_re",
          "b_im", "c_re", "c_im", "d_skip", "w_glu", "b_glu", "w_branch", "w_out", "norm_ffn_g", "w_up", "conv_w",
          "conv_b", "w_down", "norm_final_g"]
OUTPUTS = [("y_prompt", (1, TP, D)), ("y_sample", (1, TS, D)), ("pool_p", (1, 1, HIST, W)), ("pool_s", (1, 1, HIST, W)),
           ("ssm_re_p", (1, 1, G32, SS)), ("ssm_re_s", (1, 1, G32, SS)), ("ssm_im_p", (1, 1, G32, SS)),
           ("ssm_im_s", (1, 1, G32, SS)), ("k_p", (1, 1, TP, HEADS, HD)), ("k_s", (1, 1, TS, HEADS, HD)),
           ("v_p", (1, 1, TP, HEADS, HD)), ("v_s", (1, 1, TS, HEADS, HD)), ("logf_p", (1, 1, TP, HEADS)),
           ("logf_s", (1, 1, TS, HEADS)), ("conv_p", (1, 1, 2, 2 * FF)), ("conv_s", (1, 1, 2, 2 * FF))]


class Shared:
    pass


def build(nc, io, stages=99):
    m = Shared()
    scratch = lambda n, s, d=F32: nc.dram_tensor(n, s, d, kind="Internal").ap()
    m.xt_d = scratch("xt_scratch", [P, KD, T])
    m.u_d = scratch("u_scratch", [2 * W, T])
    m.qh_d, m.ql_d = scratch("qh_scratch", [W, T]), scratch("ql_scratch", [W, T])
    m.kh_d, m.kl_d = scratch("kh_scratch", [W, TK]), scratch("kl_scratch", [W, TK])
    m.vh_d, m.vl_d = scratch("vh_scratch", [TK, W]), scratch("vl_scratch", [TK, W])
    m.nc_d = scratch("nc_scratch", [HEADS, TK])
    m.yh_d, m.yl_d = scratch("yh_scratch", [3, W, T]), scratch("yl_scratch", [3, W, T])
    m.ys_d = scratch("y_ssm_scratch", [W, T])
    m.gate_d = scratch("gate_scratch", [3 * D, T])
    m.tab_d = scratch("tab_scratch", [P, G32, NTAB])
    m.k_p, m.k_s, m.v_p, m.v_s = (io[n][0, 0].rearrange("t h d -> t (h d)") for n in ("k_p", "k_s", "v_p", "v_s"))
    with ExitStack() as ctx:
        sb = lambda n, s, d=F32: ctx.enter_context(nc.sbuf_tensor(n, s, d))
        m.ident, m.ones, m.eps = sb("ident", [P, P]), sb("ones", [P, P]), sb("eps", [P, 1])
        m.vec, m.cw01, m.cw2, m.chist = sb("vec", [P, 80]), sb("cw01", [P, 88]), sb("cw2", [P, 44]), sb("chist", [P, 88])
        m.raw = sb("w_raw", [P, 2, 8, P])
        m.wh, m.wl = sb("w_hi", [P, 2, 8, P], F32R), sb("w_lo", [P, 2, 8, P], F32R)
        m.hh, m.hl = sb("act_hi", [P, KD, T], F32R), sb("act_lo", [P, KD, T], F32R)
        keep = lambda n: ctx.enter_context(nc.semaphore(n))
        m.project_ws, m.gate_ws, m.merge_ws, m.out_ws = (WeightSems(keep, n) for n in ("project", "gate", "merge", "out"))
        m.b0_ld = keep("b0_ld")
        m.pe_tick, m.pool_tick, m.dve_tick, m.sp_tick = (
            ctx.enter_context(nc.semaphore(f"{e}_tick")) for e in ("pe", "pool", "dve", "sp"))
        for n, stage in enumerate(STAGES):
            if n < stages:
                stage(nc, m, io)


def kernel(**inputs):
    import numpy as _np
    import concourse.bacc as _bacc
    from concourse.bass_utils import run_bass_kernel_spmd as _run

    nc = _bacc.Bacc("TRN2", target_bir_lowering=False, num_devices=1)
    io, arrays = {}, {}
    for name in INPUTS:
        a = _np.ascontiguousarray(inputs[name])
        arrays[f"in_{name}"] = a
        io[name] = nc.dram_tensor(f"in_{name}", a.shape, mybir.dt.from_np(a.dtype), kind="ExternalInput").ap()
    for name, shape in OUTPUTS:
        io[name] = nc.dram_tensor(f"out_{name}", shape, F32, kind="ExternalOutput").ap()
    build(nc, io)
    r = _run(nc, [arrays], core_ids=[0])
    return tuple(r.results[0][f"out_{name}"] for name, _ in OUTPUTS)
```
